# Optimizing a Trainium2 kernel written in Bass

```python
import jax, jax.numpy as jnp
from jax import lax
import numpy as np

D_MODEL = 1024
BATCH = 1
SEQ = 256
DEPTH = 1
DEC_BATCH = 8
DEC_SEQ = 4
PAST_LEN = 2048
PAGE_SIZE = 128

CHUNK = 128
A_GROUPS = 8
A_WIDTH = D_MODEL
A_GROUP_DIM = A_WIDTH // A_GROUPS
CONV_CH = D_MODEL
CONV_WIDTH = 31
N_EXPERTS = 32
TOP_K = 4
D_EXPERT = D_MODEL
SWIGLU_LIMIT = 7.0
SWIGLU_ALPHA = 1.702
EXPERT_BLOCK = 128
EPS = 1e-5
PROJ_COLS = 2 * A_WIDTH + 2 * CONV_CH + 2 * D_MODEL

kernel_name = "gated_chunk_gmlp_conformer_moe_step"

def rmsnorm(x, g):
    xf = x.astype(jnp.float32)
    y = xf * lax.rsqrt(jnp.mean(xf * xf, axis=-1, keepdims=True) + EPS)
    return (y * g.astype(jnp.float32)).astype(x.dtype)

def layernorm(x, g, b):
    xf = x.astype(jnp.float32)
    mu = jnp.mean(xf, axis=-1, keepdims=True)
    var = jnp.mean(jnp.square(xf - mu), axis=-1, keepdims=True)
    y = (xf - mu) * lax.rsqrt(var + EPS)
    return (y * g.astype(jnp.float32) + b.astype(jnp.float32)).astype(x.dtype)

def chunk_spatial_mix(v, w_s, b_s):
    bsz, t, _ = v.shape
    t_pad = -(-t // CHUNK) * CHUNK
    vp = jnp.pad(v, ((0, 0), (0, t_pad - t), (0, 0)))
    vp = vp.reshape(bsz, t_pad // CHUNK, CHUNK, A_GROUPS, A_GROUP_DIM)
    mask = jnp.tril(jnp.ones((CHUNK, CHUNK), dtype=bool))
    w = jnp.where(mask[None], w_s, jnp.zeros((), w_s.dtype)).astype(v.dtype)
    s = jnp.einsum('gij,bcjgd->bcigd', w, vp) + b_s.T.astype(v.dtype)[None, None, :, :, None]
    return s.reshape(bsz, t_pad, A_WIDTH)[:, :t]

def token_mixers(h, conv_buf, w_in, ln_v_g, ln_v_b, w_spatial, b_spatial, w_branch_a,
                 conv_w, conv_b, ln_conv_g, ln_conv_b, w_branch_b, b_branch_b,
                 b_gate_a, b_gate_b, w_out):
    p = jnp.einsum('btd,dk->btk', h, w_in)
    c0 = A_WIDTH
    c1 = 2 * A_WIDTH
    c2 = c1 + CONV_CH
    c3 = c2 + CONV_CH
    c4 = c3 + D_MODEL
    u_a, v_a, c_val, c_gate, g_a, g_b = jnp.split(p, [c0, c1, c2, c3, c4], axis=-1)
    u_a = jax.nn.gelu(u_a, approximate=False)
    v_a = layernorm(jax.nn.gelu(v_a, approximate=False), ln_v_g, ln_v_b)
    y_a = jnp.einsum('btk,kd->btd', u_a * chunk_spatial_mix(v_a, w_spatial, b_spatial), w_branch_a)
    glu = c_val * jax.nn.sigmoid(c_gate)
    padded = jnp.concatenate([conv_buf.astype(glu.dtype), glu], axis=1)
    conv = lax.conv_general_dilated(
        padded, conv_w[:, None, :].astype(padded.dtype), window_strides=(1,), padding='VALID',
        dimension_numbers=('NWC', 'WIO', 'NWC'), feature_group_count=CONV_CH) + conv_b
    y_b = jnp.einsum('btc,cd->btd', jax.nn.silu(layernorm(conv, ln_conv_g, ln_conv_b)), w_branch_b) + b_branch_b
    merged = jax.nn.sigmoid(g_a + b_gate_a) * y_a + jax.nn.sigmoid(g_b + b_gate_b) * y_b
    new_buf = padded[:, -(CONV_WIDTH - 1):]
    return jnp.einsum('btd,de->bte', merged, w_out), new_buf, v_a

def moe(h, w_router, b_router, w_up, b_up, w_down, b_down):
    bsz, t, d = h.shape
    n_tok = bsz * t
    x2 = h.reshape(n_tok, d)
    logits = jnp.einsum('td,de->te', x2.astype(jnp.float32), w_router.astype(jnp.float32)) + b_router.astype(jnp.float32)
    top_vals, top_idx = lax.top_k(logits, TOP_K)
    gates = jax.nn.softmax(top_vals, axis=-1)
    n_assign = n_tok * TOP_K
    flat_e = top_idx.reshape(-1).astype(jnp.int32)
    flat_tok = jnp.repeat(jnp.arange(n_tok, dtype=jnp.int32), TOP_K)
    flat_g = gates.reshape(-1)
    order = jnp.argsort(flat_e)
    sorted_e = flat_e[order]
    counts = jnp.bincount(flat_e, length=N_EXPERTS).astype(jnp.int32)
    start = jnp.cumsum(counts) - counts
    padded_counts = ((counts + EXPERT_BLOCK - 1) // EXPERT_BLOCK) * EXPERT_BLOCK
    padded_end = jnp.cumsum(padded_counts)
    padded_start = padded_end - padded_counts
    rank = jnp.arange(n_assign, dtype=jnp.int32) - start[sorted_e]
    dest = padded_start[sorted_e] + rank
    n_blk = -(-(n_assign + N_EXPERTS * (EXPERT_BLOCK - 1)) // EXPERT_BLOCK)
    n_rows = n_blk * EXPERT_BLOCK
    row_tok = jnp.zeros((n_rows,), jnp.int32).at[dest].set(flat_tok[order])
    row_gate = jnp.zeros((n_rows,), jnp.float32).at[dest].set(flat_g[order])
    block_expert = jnp.clip(
        jnp.searchsorted(padded_end, jnp.arange(n_blk, dtype=jnp.int32) * EXPERT_BLOCK, side='right'),
        0, N_EXPERTS - 1)
    xs = x2[row_tok].reshape(n_blk, EXPERT_BLOCK, d)

    def expert_block(args):
        xb, e = args
        gu = xb @ w_up[e] + b_up[e]
        gate, up = gu[:, :D_EXPERT], gu[:, D_EXPERT:]
        gate = jnp.minimum(gate, SWIGLU_LIMIT)
        up = jnp.clip(up, -SWIGLU_LIMIT, SWIGLU_LIMIT)
        act = (up + 1.0) * (gate * jax.nn.sigmoid(SWIGLU_ALPHA * gate))
        return act @ w_down[e] + b_down[e]

    out = lax.map(expert_block, (xs, block_expert)).reshape(n_rows, d)
    y = jax.ops.segment_sum(out * row_gate[:, None].astype(out.dtype), row_tok, num_segments=n_tok)
    return y.reshape(bsz, t, d).astype(h.dtype)

def layer(x, conv_buf, norm_mix_g, w_in, ln_v_g, ln_v_b, w_spatial, b_spatial, w_branch_a,
          conv_w, conv_b, ln_conv_g, ln_conv_b, w_branch_b, b_branch_b, b_gate_a, b_gate_b,
          w_out, norm_ffn_g, w_router, b_router, w_up, b_up, w_down, b_down):
    mix, new_buf, v_rows = token_mixers(
        rmsnorm(x, norm_mix_g), conv_buf, w_in, ln_v_g, ln_v_b, w_spatial, b_spatial, w_branch_a,
        conv_w, conv_b, ln_conv_g, ln_conv_b, w_branch_b, b_branch_b, b_gate_a, b_gate_b, w_out)
    x = x + mix
    x = x + moe(rmsnorm(x, norm_ffn_g), w_router, b_router, w_up, b_up, w_down, b_down)
    return x, new_buf, v_rows

def setup_inputs(seed: int = 0) -> dict:
    key = jax.random.key(seed)
    ks = iter(jax.random.split(key, 40))

    def nrm(shape, scale):
        return jax.random.normal(next(ks), shape, jnp.float32) * scale

    L, D, E, F = DEPTH, D_MODEL, N_EXPERTS, D_EXPERT
    return {
        "x_prompt": nrm((BATCH, SEQ, D), 1.0),
        "x_sample": nrm((DEC_BATCH, DEC_SEQ, D), 1.0),
        "cache_conv": nrm((L, DEC_BATCH, CONV_WIDTH - 1, CONV_CH), 0.5),
        "norm_mix_g": 1.0 + nrm((L, D), 0.02),
        "w_in": nrm((L, D, PROJ_COLS), D ** -0.5),
        "ln_v_g": 1.0 + nrm((L, A_WIDTH), 0.02),
        "ln_v_b": nrm((L, A_WIDTH), 0.02),
        "w_spatial": nrm((L, A_GROUPS, CHUNK, CHUNK), CHUNK ** -0.5),
        "b_spatial": 1.0 + nrm((L, A_GROUPS, CHUNK), 0.02),
        "w_branch_a": nrm((L, A_WIDTH, D), A_WIDTH ** -0.5),
        "conv_w": nrm((L, CONV_WIDTH, CONV_CH), CONV_WIDTH ** -0.5),
        "conv_b": nrm((L, CONV_CH), 0.02),
        "ln_conv_g": 1.0 + nrm((L, CONV_CH), 0.02),
        "ln_conv_b": nrm((L, CONV_CH), 0.02),
        "w_branch_b": nrm((L, CONV_CH, D), CONV_CH ** -0.5),
        "b_branch_b": nrm((L, D), 0.02),
        "b_gate_a": nrm((L, D), 0.02),
        "b_gate_b": nrm((L, D), 0.02),
        "w_out": nrm((L, D, D), D ** -0.5),
        "norm_ffn_g": 1.0 + nrm((L, D), 0.02),
        "w_router": nrm((L, D, E), D ** -0.5),
        "b_router": nrm((L, E), 0.01),
        "w_up": nrm((L, E, D, 2 * F), D ** -0.5),
        "b_up": nrm((L, E, 2 * F), 0.02),
        "w_down": nrm((L, E, F, D), F ** -0.5),
        "b_down": nrm((L, E, D), 0.02),
        "norm_final_g": 1.0 + nrm((D,), 0.02),
    }

def reference(x_prompt, x_sample, cache_conv, norm_mix_g, w_in, ln_v_g, ln_v_b, w_spatial,
              b_spatial, w_branch_a, conv_w, conv_b, ln_conv_g, ln_conv_b, w_branch_b,
              b_branch_b, b_gate_a, b_gate_b, w_out, norm_ffn_g, w_router, b_router, w_up,
              b_up, w_down, b_down, norm_final_g):
    xp, xs = x_prompt, x_sample
    conv_p, conv_s, v_s = [], [], []
    for l in range(DEPTH):
        lp = (norm_mix_g[l], w_in[l], ln_v_g[l], ln_v_b[l], w_spatial[l], b_spatial[l],
              w_branch_a[l], conv_w[l], conv_b[l], ln_conv_g[l], ln_conv_b[l], w_branch_b[l],
              b_branch_b[l], b_gate_a[l], b_gate_b[l], w_out[l], norm_ffn_g[l], w_router[l],
              b_router[l], w_up[l], b_up[l], w_down[l], b_down[l])
        buf0 = jnp.zeros((xp.shape[0], CONV_WIDTH - 1, CONV_CH), xp.dtype)
        xp, bp, _ = layer(xp, buf0, *lp)
        xs, bs, vs = layer(xs, cache_conv[l], *lp)
        conv_p.append(bp)
        conv_s.append(bs)
        v_s.append(vs)
    y_prompt = rmsnorm(xp, norm_final_g)
    y_sample = rmsnorm(xs, norm_final_g)
    conv_state_prompt = jnp.stack(conv_p)
    conv_state_sample = jnp.stack(conv_s)
    chunk_v_sample = jnp.stack(v_s)
    return (y_prompt, y_sample, conv_state_prompt, conv_state_sample, chunk_v_sample)


_drawn_inputs = setup_inputs


def setup_inputs(seed=0):
    import zlib

    import numpy as np

    out = dict(_drawn_inputs(seed))
    spreads = {}
    factors = {'b_gate_a': 3.257, 'b_up': 5.465, 'b_down': 6.231, 'norm_final_g': 2.784}
    for name, (base, spread) in spreads.items():
        noise = np.random.default_rng([zlib.crc32(name.encode()), seed]).standard_normal(out[name].shape)
        drawn = base * np.exp(spread * noise) if base else spread * noise
        out[name] = __import__('jax').numpy.asarray(drawn.astype(out[name].dtype))
    for name, factor in factors.items():
        out[name] = (out[name] * factor).astype(out[name].dtype)
    return out
```

```python
import concourse.bass as bass
from concourse import mybir
from contextlib import ExitStack

F32 = mybir.dt.float32
I32 = mybir.dt.int32
ALU = mybir.AluOpType
ACT = mybir.ActivationFunctionType
AX = mybir.AxisListType

P = 128
D = 1024
KC = D // P
SEQ = 256
DB, DS = 8, 4
NS = DB * DS
T = SEQ + NS
NT = 3
ROWS = [P, P, NS]
W = 31
HIST = W - 1
SEG = HIST + DS
CB = HIST + SEQ + DB * SEG
G = 8
NE = 32
TOPK = 4
BLK = 64
MAX_ROUNDS = -(-T // BLK)
TBL = (MAX_ROUNDS + 1) * NE
SLOTS = 12
SLOT = 2048
UP_SLOTS = 8
MIX_BLOCKS = 36
FILLS = MIX_BLOCKS // SLOTS
EPS = 1e-5
LIMIT = 7.0
ALPHA = 1.702
ABSENT = 4096.0
SENTINEL = 3.0e38


def token_slices(tt):
    return slice(tt * P, tt * P + ROWS[tt])


def mix_block_source(n, w_in, w_a, w_b, w_out):
    c0 = 2 * D
    if n < 8:
        start = c0 + (n % 2) * D + (n // 2) * 256
        src = w_in[0, :, start:start + 256]
    elif n < 24:
        base = [D, 0, 4 * D, 5 * D][(n - 8) // 4]
        start = base + (n % 4) * 256
        src = w_in[0, :, start:start + 256]
    else:
        w = [w_b, w_a, w_out][(n - 24) // 4]
        src = w[0, :, (n % 4) * 256:(n % 4) * 256 + 256]
    return src.rearrange("(k p) n -> p k n", p=P)


def hybrid_layer(nc, a, out):
    with ExitStack() as ctx:
        def sb(name, shape, dt=F32):
            return ctx.enter_context(nc.sbuf_tensor(name, shape, dt))

        def sem(name):
            return ctx.enter_context(nc.semaphore(name))

        ring = sb("ring", [P, SLOTS, SLOT])
        xt = sb("xt", [P, NT, D])
        stage = sb("stage", [P, NT, D])
        hT = sb("hT", [P, KC, T])
        ident = sb("ident", [P, P])
        mean_w = sb("mean_w", [P, P])
        ones = sb("ones", [P, P])
        below = sb("below", [P, P])
        slot_ids = sb("slot_ids", [P, 2, BLK])
        cols = sb("cols", [P, 8, KC])
        convw = sb("convw", [P, KC, W])
        vecrows = sb("vecrows", [BLK, P])
        bupT = sb("bupT", [P, NE, 2 * KC])
        wr = sb("wr", [P, KC, NE])
        br = sb("br", [P, NE])
        spb = sb("spb", [P, G, P])
        WT = sb("WT", [P, G, P])
        WS = sb("WS", [NS, G, NS])
        bmask = sb("bmask", [NS, DB])
        rep4 = sb("rep4", [DS, DB, DS])
        tmpc = sb("tmpc", [P, 2, T])
        eps_col = sb("eps_col", [P, 1])
        glu_tail = sb("glu_tail", [P, KC, NS])
        ss = sb("ss", [P, 16])
        bnst = sb("bnst", [P, NT, 2, 6])
        mv = sb("mv", [P, NT, 2])
        n_pairs = sb("n_pairs", [P, 1], I32)
        big = sb("big", [P, KC * CB])
        R1 = sb("R1", [P, KC * T])
        R2 = sb("R2", [P, KC * T])
        R3 = sb("R3", [P, KC * T])
        R4 = sb("R4", [P, KC * T])

        def view(t, c):
            return t[:, :].rearrange("p (c t) -> p c t", c=c)

        convbuf = view(big, KC)
        cprompt = convbuf[:, :, 0:HIST + SEQ]
        csample = convbuf[:, :, HIST + SEQ:CB].rearrange("p c (b s) -> p c b s", b=DB)
        conv = view(R1, KC)
        uT = view(R2, KC)
        gaT = view(R3, KC)
        gbT = view(R4, KC)
        sq = big[:, 0:KC * T].rearrange("p (c t) -> p c t", c=KC)
        bup_rows = R1[0:NE, 0:2 * D]
        wsp = R2[:, 0:G * P].rearrange("p (g j) -> p g j", g=G)
        cw_rows = R2[0:W, G * P:G * P + D]
        cache_rows = R3[0:4 * HIST, 0:2 * D].rearrange("p (h c) -> p h c", h=2)
        lnv_g = R4[:, 0:D]
        lnv_b = R4[:, D:2 * D]
        st_rows = R3[0:NS, 0:2 * D].rearrange("p (q c) -> p q c", q=2)
        prod = sb("prod", [P, DB, DS, W])

        pos = {"big": 0, "R1": 0, "R2": 0, "R4": 0}
        regs = {"big": big, "R1": R1, "R2": R2, "R4": R4}

        def carve(region, n, rows=P):
            lo = pos[region]
            pos[region] = lo + n
            assert pos[region] <= regs[region].shape[1]
            return regs[region][0:rows, lo:lo + n]

        xT = [carve("big", KC * BLK).rearrange("p (k t) -> p k t", k=KC) for _ in range(2)]
        raw_g, raw_u = carve("big", 512), carve("big", 512)
        g1, sg, u1, gs = (carve("big", 512) for _ in range(4))
        actT = carve("R1", 512)
        out_sb = carve("R1", 512)
        sel = [carve("R1", NT * BLK).rearrange("p (t j) -> p t j", t=NT) for _ in range(2)]
        comb = [carve("R1", NT * P).rearrange("p (t q j) -> p t q j", t=NT, q=2) for _ in range(2)]
        lg = carve("R1", NT * NE).rearrange("p (t e) -> p t e", t=NT)
        combT = [carve("R2", NT * P) for _ in range(2)]
        tbl_rank = carve("R2", NT * TBL).rearrange("p (t i) -> p t i", t=NT)
        tbl_gate = carve("R2", NT * TBL).rearrange("p (t i) -> p t i", t=NT)
        gateT = carve("R4", T, NE)
        bdown = carve("R4", D, NE)
        lx = carve("R4", NT * (NE + 8)).rearrange("p (t e) -> p t e", t=NT)
        lr = carve("R4", NT * (NE + 8)).rearrange("p (t e) -> p t e", t=NT)
        top8 = carve("R4", NT * 8).rearrange("p (t e) -> p t e", t=NT)
        want8 = carve("R4", NT * 8).rearrange("p (t e) -> p t e", t=NT)
        mask = carve("R4", NT * NE).rearrange("p (t e) -> p t e", t=NT)
        gates = carve("R4", NT * NE).rearrange("p (t e) -> p t e", t=NT)
        rankm = carve("R4", NT * NE).rearrange("p (t e) -> p t e", t=NT)
        fing = R3[:, 0:D]

        bank = [ctx.enter_context(nc.psum_tensor(f"bank{i}", [P, 512], F32)) for i in range(8)]
        U0, U1, T0, T1, XB, DN, Y0, Y1 = bank

        slot_full = [sem(f"slot_full{k}") for k in range(SLOTS)]
        x_in, vec_in, cw_in, cache_in, wsp_in, bup_in, lnv_in, wr_in = (
            sem(n) for n in ("x_in", "vec_in", "cw_in", "cache_in", "wsp_in", "bup_in", "lnv_in", "wr_in"))
        bdown_in, fing_in = sem("bdown_in"), sem("fing_in")
        stored, v_stored, st_stored = sem("stored"), sem("v_stored"), sem("st_stored")
        old_rows_stored = sem("old_rows_stored")
        slots_used = sem("slots_used")
        const_step, const_ready = sem("const_step"), sem("const_ready")
        pads_zero = sem("pads_zero")
        pe_early, evac_early = sem("pe_early"), sem("evac_early")
        ws_raw, ws_ready, wt_masked = sem("ws_raw"), sem("ws_ready"), sem("wt_masked")
        squared, xs_ready = sem("squared"), sem("xs_ready")
        x_transposed, hT_ready = sem("x_transposed"), sem("hT_ready")
        c_proj, gate_sig, glu_ready = sem("c_proj"), sem("gate_sig"), sem("glu_ready")
        proj, act_evac = sem("proj"), sem("act_evac")
        v_transposed, v_rows = sem("v_transposed"), sem("v_rows")
        tail_packed = sem("tail_packed")
        st_transposed, st_ready = sem("st_transposed"), sem("st_ready")
        prod_ready, prod_used = sem("prod_ready"), sem("prod_used")
        conv_done, mean_ready, sq_ready, var_ready, conv_normed, silu_done = (
            sem(n) for n in ("conv_done", "mean_ready", "sq_ready", "var_ready", "conv_normed", "silu_done"))
        centered = sem("centered")
        v_normed = sem("v_normed")
        sp_ready, sp_evac = sem("sp_ready"), sem("sp_evac")
        yb_ready, yb_evac = sem("yb_ready"), sem("yb_evac")
        ya_ready, ya_evac = sem("ya_ready"), sem("ya_evac")
        mo_ready, mo_evac = sem("mo_ready"), sem("mo_evac")
        mo_transposed, x2_ready = sem("mo_transposed"), sem("x2_ready")
        v_stats, rooted = sem("v_stats"), sem("rooted")
        squared2, xs2_ready, x2_transposed, h2T_ready = (
            sem(n) for n in ("squared2", "xs2_ready", "x2_transposed", "h2T_ready"))
        logits_ready, shifted, exped, routed = (
            sem(n) for n in ("logits_ready", "shifted", "exped", "routed"))
        rank_ready, gT_ready, gT_evac, bd_ready, pairs_known = (
            sem(n) for n in ("rank_ready", "gT_ready", "gT_evac", "bd_ready", "pairs_known"))
        sel_ready, gathered, xT_ready = sem("sel_ready"), sem("gathered"), sem("xT_ready")
        raw_g_ready, raw_u_ready, turned = sem("raw_g_ready"), sem("raw_u_ready"), sem("turned")
        g1_ready, sig_ready, act_ready = sem("g1_ready"), sem("sig_ready"), sem("act_ready")
        combT_turned, combT_ready = sem("combT_turned"), sem("combT_ready")
        out_ready, combined, y_added = sem("out_ready"), sem("combined"), sem("y_added")
        squared3, y_ready = sem("squared3"), sem("y_ready")
        dve_step, act_step = sem("dve_step"), sem("act_step")

        NORM_MIX, GATE_A, GATE_B, B_B, CONV_B, LNC_G, LNC_B, NORM_FFN = range(8)
        vec_names = ["norm_mix_g", "b_gate_a", "b_gate_b", "b_branch_b", "conv_b", "ln_conv_g",
                     "ln_conv_b", "norm_ffn_g"]

        def col(v, c):
            return cols[:, v, c:c + 1]

        def make_link(eng, s):
            n = [0]

            def link(ins, base=None):
                n[0] += 1
                ins.then_inc(s, 1)
                eng.wait_ge(s, n[0] if base is None else base + n[0])
            link.count = n
            return link

        def mix_block_used(n):
            if n < 8:
                return c_proj, 2 * n + 2
            if n < 24:
                return proj, 2 * (n - 8) + 2
            return (yb_ready, ya_ready, mo_ready)[(n - 24) // 4], 2 * (n % 4) + 2

        LINKS = 8
        dev_inv = prod[:].rearrange("p b t k -> p (b t k)")[:, 0:T]
        row_banks = ((Y0, Y1), (U0, U1), (Y0, Y1))

        def root(dst, src, scale):
            nc.scalar.activation(dst, src, ACT.Sqrt, bias=eps_col[0:src.shape[0], :], scale=scale
                                 ).then_inc(rooted, 1)

        def copy_v(act, c):
            b = bank[4 + c % 2]
            act.wait_ge(v_transposed, c + 1)
            nc.scalar.copy(stage[:, 0:2, c * P:(c + 1) * P], b[:, 0:2 * P].rearrange("p (t d) -> p t d", t=2)
                           ).then_inc(v_rows, 1)
            nc.scalar.copy(stage[0:NS, 2, c * P:(c + 1) * P], b[0:NS, 2 * P:3 * P]).then_inc(v_rows, 1)

        def add_outputs(dve, done):
            for tt in range(NT):
                r = ROWS[tt]
                dve.wait_ge(combined, done + (tt + 1))
                for h in range(2):
                    dst = xt[0:r, tt, h * 512:(h + 1) * 512]
                    ins = nc.vector.tensor_tensor(dst, dst, row_banks[tt][h][0:r, :], ALU.add)
                ins.then_inc(y_added, 1)

        def turn_v(pe, tr, c):
            pe.wait_ge(act_evac, c + 1)
            if c >= 2:
                pe.wait_ge(v_rows, 2 * (c - 1))
            for tt in range(NT):
                ins = tr(bank[4 + c % 2][0:ROWS[tt], tt * P:(tt + 1) * P], tmpc[:, c % 2, token_slices(tt)])
            ins.then_inc(v_transposed, 1)

        def turn_mixed(pe, tr, c):
            pe.wait_ge(mo_evac, c + 1)
            if c >= 4:
                pe.wait_ge(x2_ready, c - 3)
            for tt in range(NT):
                ins = tr(bank[4 + c % 4][0:ROWS[tt], tt * P:(tt + 1) * P], tmpc[:, c % 2, token_slices(tt)])
            ins.then_inc(mo_transposed, 1)

        block = ctx.enter_context(nc.Block())

        @block.sync
        def _(sp):
            for n in range(MIX_BLOCKS):
                if n >= SLOTS:
                    sp.wait_ge(*mix_block_used(n - SLOTS))
                sp.dma_start(ring[:, n % SLOTS, :].rearrange("p (k n) -> p k n", k=KC),
                             mix_block_source(n, a["w_in"], a["w_branch_a"], a["w_branch_b"], a["w_out"])
                             ).then_inc(slot_full[n % SLOTS], 16)

            def load_expert(e, used):
                for k in range(SLOTS):
                    if used is None:
                        sp.wait_ge(*mix_block_used(MIX_BLOCKS - SLOTS + k))
                    else:
                        sp.wait_ge(slots_used, used + k)
                    if k < UP_SLOTS:
                        src = a["w_up"][0, bass.ds(e, 1), k * P:(k + 1) * P, :].rearrange("e p n -> (e p) n")
                        dst = ring[:, k, :]
                    else:
                        j = k - UP_SLOTS
                        src = a["w_down"][0, bass.ds(e, 1), j * 256:(j + 1) * 256, :].rearrange(
                            "e (h p) n -> p (e h) n", p=P)
                        dst = ring[:, k, :].rearrange("p (h n) -> p h n", h=2)
                    sp.dma_start(dst, src).then_inc(slot_full[k], 16)

            load_expert(0, None)
            load_expert(1, 1)
            sp.wait_ge(pairs_known, 1)
            pairs = sp.value_load(n_pairs[0:1, 0:1], min_val=NE // 2, max_val=MAX_ROUNDS * NE // 2)
            expert_reg = [sp.alloc_register(f"expert{s}") for s in range(2)]
            with sp.Fori(1, pairs) as ip:
                for s in range(2):
                    sp.reg_alu(expert_reg[s], ip * 2 + s, NE - 1, ALU.bitwise_and)
                experts = [sp.snap(r, min_val=0, max_val=NE - 1) for r in expert_reg]
                for s in range(2):
                    load_expert(experts[s], ip * (2 * SLOTS) + ((s - 1) * SLOTS + 1))
            for tt in range(NT):
                sp.wait_ge(y_ready, tt + 1)
                dst = out["y_sample"].rearrange("b t d -> (b t) d") if tt == 2 else \
                    out["y_prompt"][0, tt * P:(tt + 1) * P, :]
                sp.dma_start(dst, xt[0:ROWS[tt], tt, :]).then_inc(stored, 16)
            sp.wait_ge(stored, 16 * NT)
            sp.wait_ge(old_rows_stored, 16)
            sp.wait_ge(v_stored, 16)
            sp.wait_ge(st_stored, 16 * (1 + DB))

        @block.gpsimd
        def _(pool):
            nc.gpsimd.memset(xt[:, 2, :], 0.0).then_inc(pads_zero, 1)
            nc.gpsimd.memset(cprompt[:, :, 0:HIST], 0.0).then_inc(pads_zero, 1)
            nc.gpsimd.memset(ident[:], 0.0).then_inc(const_step, 1)
            nc.gpsimd.memset(ones[:], 1.0).then_inc(const_step, 1)
            nc.gpsimd.memset(below[:], 1.0).then_inc(const_step, 1)
            nc.gpsimd.memset(mean_w[:], 1.0 / D).then_inc(const_step, 1)
            nc.gpsimd.memset(bmask[:], 1.0).then_inc(const_step, 1)
            nc.gpsimd.memset(eps_col[:], EPS).then_inc(const_ready, 1)
            nc.gpsimd.iota(slot_ids[:], [[0, 2], [1, BLK]], base=0, channel_multiplier=0,
                           allow_small_or_imprecise_dtypes=True).then_inc(const_step, 1)
            pool.wait_ge(const_step, 6)
            nc.gpsimd.affine_select(out=ident[:], in_=ident[:], compare_op=ALU.not_equal, fill=1.0, base=0,
                                    pattern=[[-1, P]], channel_multiplier=1).then_inc(const_ready, 1)
            nc.gpsimd.affine_select(out=below[:], in_=below[:], compare_op=ALU.is_gt, fill=0.0, base=0,
                                    pattern=[[1, P]], channel_multiplier=-1).then_inc(const_ready, 1)
            nc.gpsimd.affine_select(out=bmask[:], in_=bmask[:], compare_op=ALU.is_ge, fill=0.0, base=0,
                                    pattern=[[-DS, DB]], channel_multiplier=1).then_inc(const_step, 1)
            pool.wait_ge(const_step, 7)
            nc.gpsimd.affine_select(out=bmask[:], in_=bmask[:], compare_op=ALU.is_ge, fill=0.0, base=DS - 1,
                                    pattern=[[DS, DB]], channel_multiplier=-1).then_inc(const_ready, 1)
            for_rows = a["cache_conv"][0, :, DS:HIST, :]
            pool.dma_start(out["conv_state_sample"][0, :, 0:HIST - DS, :], for_rows
                           ).then_inc(old_rows_stored, 16)
            for c in range(KC):
                pool.wait_ge(glu_ready, c + 1)
                if c == 0:
                    pool.wait_ge(evac_early, 3)
                if c == KC - 1:
                    nc.gpsimd.tensor_copy(glu_tail[:].rearrange("p c (b t) -> p c b t", b=DB),
                                          csample[:, :, :, HIST:SEG]).then_inc(tail_packed, 1)
                if c >= 1:
                    pool.wait_ge(prod_used, c)
                for t in range(DS):
                    nc.gpsimd.tensor_tensor(prod[:, :, t, :], csample[:, c, :, t:t + W],
                                            convw[:, c:c + 1, :].to_broadcast([P, DB, W]), ALU.mult
                                            ).then_inc(prod_ready, 1)
                if c == 4:
                    pool.wait_ge(evac_early, 5)
                    nc.gpsimd.affine_select(out=WT[:], in_=WT[:], compare_op=ALU.is_ge, fill=0.0, base=0,
                                            pattern=[[0, G], [1, P]], channel_multiplier=-1
                                            ).then_inc(wt_masked, 1)

        @block.scalar
        def _(act):
            act.wait_ge(pads_zero, 1)
            act.dma_start(xt[:, 0:2, :], a["x_prompt"][0].rearrange("(t p) d -> p t d", p=P)).then_inc(x_in, 16)
            act.dma_start(xt[0:NS, 2, :], a["x_sample"].rearrange("b t d -> (b t) d")).then_inc(x_in, 16)
            for v, name in enumerate(vec_names):
                act.dma_start(vecrows[v * KC:(v + 1) * KC, :], a[name][0].rearrange("(c p) -> c p", p=P)
                              ).then_inc(vec_in, 16)
            act.dma_start(cw_rows, a["conv_w"][0]).then_inc(cw_in, 16)
            cache = a["cache_conv"][0].rearrange("b h c -> (b h) c")
            for h in range(2):
                act.dma_start(cache_rows[:, h, :], cache[h * 4 * HIST:(h + 1) * 4 * HIST, :]).then_inc(cache_in, 16)
            act.dma_start(wsp, a["w_spatial"][0].rearrange("g i j -> i g j")).then_inc(wsp_in, 16)
            act.dma_start(bup_rows, a["b_up"][0]).then_inc(bup_in, 16)
            act.dma_start(lnv_g, a["ln_v_g"].to_broadcast([P, D])).then_inc(lnv_in, 16)
            act.dma_start(lnv_b, a["ln_v_b"].to_broadcast([P, D])).then_inc(lnv_in, 16)
            act.dma_start(spb[:].rearrange("p g i -> p (g i)"),
                          a["b_spatial"].rearrange("l g i -> l (g i)").to_broadcast([P, D])).then_inc(lnv_in, 16)
            act.dma_start(wr[:], a["w_router"][0].rearrange("(k p) e -> p k e", p=P)).then_inc(wr_in, 16)
            act.dma_start(br[:], a["b_router"].to_broadcast([P, NE])).then_inc(wr_in, 16)
            act.wait_ge(x_in, 32)
            for tt in range(NT):
                nc.scalar.activation(stage[:, tt, :], xt[:, tt, :], ACT.Square, accum_out=ss[:, tt:tt + 1]
                                     ).then_inc(squared, 1)
            act.wait_ge(const_ready, 4)
            act.wait_ge(squared, NT)
            root(ss[:, 4:4 + NT], ss[:, 0:NT], 1.0 / D)
            act.wait_ge(evac_early, 1)
            for c in range(KC):
                act.wait_ge(x_transposed, c + 1)
                nc.scalar.mul(hT[:, c, :], bank[c][:, 0:T], col(NORM_MIX, c)).then_inc(hT_ready, 1)
            for c in range(KC):
                act.wait_ge(c_proj, 4 * (c // 2) + 3 + c % 2)
                if c >= 2:
                    act.wait_ge(glu_ready, c - 1)
                nc.scalar.activation(tmpc[:, c % 2, :], bank[4 * (c // 2 % 2) + 2 + c % 2][:, 0:T], ACT.Sigmoid
                                     ).then_inc(gate_sig, 1)
            for n in range(4 * KC):
                kind, c = divmod(n, KC)
                act.wait_ge(proj, n + 1)
                src = bank[n % 4][:, 0:T]
                if kind == 0:
                    if c < 2:
                        act.wait_ge(glu_ready, KC - 1 + c)
                    else:
                        act.wait_ge(v_transposed, c - 1)
                    nc.scalar.activation(tmpc[:, c % 2, :], src, ACT.Gelu).then_inc(act_evac, 1)
                    if c >= 1:
                        copy_v(act, c - 1)
                elif kind == 1:
                    if c == 0:
                        copy_v(act, KC - 1)
                    if c == 0:
                        act.wait_ge(evac_early, 5)
                    nc.scalar.activation(uT[:, c, :], src, ACT.Gelu).then_inc(act_evac, 1)
                    if c == 0:
                        for h in range(2):
                            act.wait_ge(st_transposed, 4 * (h + 1))
                            nc.scalar.copy(st_rows[0:HIST, 0, h * 512:(h + 1) * 512], bank[6][0:HIST, :]
                                           ).then_inc(st_ready, 1)
                        for h in range(2):
                            act.wait_ge(st_transposed, 8 + 4 * (h + 1))
                            nc.scalar.copy(st_rows[:, 1, h * 512:(h + 1) * 512], bank[7][0:NS, :]
                                           ).then_inc(st_ready, 1)
                        act.wait_ge(st_ready, 4)
                        act.dma_start(out["conv_state_prompt"][0, 0], st_rows[0:HIST, 0, :]).then_inc(st_stored, 16)
                        for b in range(DB):
                            act.dma_start(out["conv_state_sample"][0, b, HIST - DS:HIST, :],
                                          st_rows[b * DS:(b + 1) * DS, 1, :]).then_inc(st_stored, 16)
                elif kind == 2:
                    if c == 0:
                        act.wait_ge(st_stored, 16 * (1 + DB))
                        act.wait_ge(v_stats, 1)
                        root(ss[:, 8:10], mv[:, 0:2, 1], 1.0)
                        root(ss[0:NS, 10:11], mv[0:NS, 2, 1:2], 1.0)
                        act.wait_ge(centered, 1)
                        nc.scalar.activation(sq, conv, ACT.Square).then_inc(sq_ready, 1)
                    nc.scalar.activation(gaT[:, c, :], src, ACT.Sigmoid, bias=col(GATE_A, c)).then_inc(act_evac, 1)
                else:
                    if c == 0:
                        act.wait_ge(var_ready, 1)
                        root(dev_inv, bank[5][:, 0:T], 1.0)
                        act.wait_ge(v_normed, NT)
                    nc.scalar.activation(gbT[:, c, :], src, ACT.Sigmoid, bias=col(GATE_B, c)).then_inc(act_evac, 1)
            act.wait_ge(v_normed, NT)
            act.dma_start(out["chunk_v_sample"].rearrange("l b t d -> (l b t) d"), stage[0:NS, 2, :]
                          ).then_inc(v_stored, 16)
            act.wait_ge(conv_normed, 1)
            for c in range(KC):
                nc.scalar.activation(conv[:, c, :], conv[:, c, :], ACT.Silu, bias=col(LNC_B, c),
                                     scale=col(LNC_G, c)).then_inc(silu_done, 1)
            for c in range(KC):
                act.wait_ge(mo_ready, c + 1)
                if c >= 2:
                    act.wait_ge(mo_transposed, c - 1)
                nc.scalar.copy(tmpc[:, c % 2, :], bank[c % 4][:, 0:T]).then_inc(mo_evac, 1)
            act.wait_ge(x2_ready, KC)
            act.dma_start(bdown, a["b_down"][0]).then_inc(bdown_in, 16)
            act.dma_start(fing, a["norm_final_g"].rearrange("(l d) -> l d", l=1).to_broadcast([P, D])
                          ).then_inc(fing_in, 16)
            act.wait_ge(v_stored, 16)
            for tt in range(NT):
                nc.scalar.activation(stage[:, tt, :], xt[:, tt, :], ACT.Square, accum_out=ss[:, tt:tt + 1]
                                     ).then_inc(squared2, 1)
            act.wait_ge(squared2, NT)
            root(ss[:, 4:4 + NT], ss[:, 0:NT], 1.0 / D)
            for c in range(KC):
                act.wait_ge(x2_transposed, c + 1)
                nc.scalar.mul(hT[:, c, :], bank[c][:, 0:T], col(NORM_FFN, c)).then_inc(h2T_ready, 1)
            act.wait_ge(shifted, 1)
            nc.scalar.activation(gates[:], gates[:], ACT.Exp).then_inc(exped, 1)
            act.wait_ge(gT_ready, 1)
            nc.scalar.copy(gateT, bank[5][0:NE, 0:T]).then_inc(gT_evac, 1)
            act.wait_ge(pairs_known, 1)
            pairs = act.value_load(n_pairs[0:1, 0:1], min_val=NE // 2, max_val=MAX_ROUNDS * NE // 2)
            with act.Fori(0, pairs) as ip:
                for s in range(2):
                    i = ip * 2 + s
                    used = ip * (2 * SLOTS) + s * SLOTS
                    act.wait_ge(slots_used, used + UP_SLOTS)
                    nc.scalar.copy(raw_g, U0[:, :]).then_inc(raw_g_ready, 1)
                    act.wait_ge(g1_ready, i + 1)
                    nc.scalar.activation(sg, g1, ACT.Sigmoid, scale=ALPHA).then_inc(sig_ready, 1)
                    act.wait_ge(combT_turned, i + 1)
                    nc.scalar.copy(combT[s], XB[:, 0:NT * P]).then_inc(combT_ready, 1)
                    act.wait_ge(slots_used, used + SLOTS)
                    act.wait_ge(combined, ip * NT * 2 + NT * (s + 1))
                    nc.scalar.copy(out_sb, DN[:, :]).then_inc(out_ready, 1)
            for tt in range(NT):
                act.wait_ge(y_added, pairs * (2 * NT) + (NT + tt + 1))
                nc.scalar.activation(stage[:, tt, :], xt[:, tt, :], ACT.Square, accum_out=ss[:, tt:tt + 1]
                                     ).then_inc(squared3, 1)
            act.wait_ge(squared3, NT)
            root(ss[:, 4:4 + NT], ss[:, 0:NT], 1.0 / D)

        @block.vector
        def _(dve):
            link = make_link(dve, dve_step)
            V = nc.vector

            dve.wait_ge(const_ready, 4)
            V.tensor_copy(rep4[:], ident[0:DS, 0:DS].unsqueeze(1).to_broadcast([DS, DB, DS])
                          ).then_inc(ws_raw, 1)
            dve.wait_ge(pe_early, 1)
            V.tensor_copy(cols[:].rearrange("p v c -> p (v c)"), bank[7][:, 0:8 * KC]).then_inc(evac_early, 1)
            dve.wait_ge(rooted, 1)
            link(V.reciprocal(ss[:, 4:4 + NT], ss[:, 4:4 + NT]))
            for tt in range(NT):
                V.tensor_scalar(stage[:, tt, :], xt[:, tt, :], ss[:, 4 + tt:5 + tt], None, ALU.mult
                                ).then_inc(xs_ready, 1)
            dve.wait_ge(pe_early, 2)
            for c in range(KC):
                ins = V.tensor_copy(csample[:, c, :, 0:HIST],
                                    bank[4 + c // 2][:, (c % 2) * DB * HIST:(c % 2 + 1) * DB * HIST]
                                    .rearrange("p (b h) -> p b h", b=DB))
            ins.then_inc(evac_early, 1)
            dve.wait_ge(pe_early, 3)
            V.tensor_copy(convw[:], bank[4][:, 0:KC * W].rearrange("p (c k) -> p c k", c=KC)
                          ).then_inc(evac_early, 1)
            dve.wait_ge(pe_early, 4)
            V.tensor_copy(bupT[:].rearrange("p e f -> p f e"), bank[5][:, :].rearrange("p (f e) -> p f e", e=NE)
                          ).then_inc(evac_early, 1)
            dve.wait_ge(pe_early, 5)
            for h in range(2):
                ins = V.tensor_copy(WT[:, 4 * h:4 * h + 4, :],
                                    bank[6 + h][:, :].rearrange("p (g i) -> p g i", g=4))
            ins.then_inc(evac_early, 1)

            def glu(c):
                dve.wait_ge(gate_sig, c + 1)
                b = bank[4 * (c // 2 % 2) + c % 2]
                V.tensor_tensor(cprompt[:, c, HIST:HIST + SEQ], b[:, 0:SEQ], tmpc[:, c % 2, 0:SEQ], ALU.mult)
                V.tensor_tensor(csample[:, c, :, HIST:SEG], b[:, SEQ:T].rearrange("p (b t) -> p b t", b=DB),
                                tmpc[:, c % 2, SEQ:T].rearrange("p (b t) -> p b t", b=DB), ALU.mult
                                ).then_inc(glu_ready, 1)

            def convolve(c):
                if c == 0:
                    dve.wait_ge(pads_zero, 2)
                dve.wait_ge(glu_ready, c + 1)
                acc = conv[:, c, 0:SEQ]
                link(V.tensor_scalar(acc, cprompt[:, c, 0:SEQ], convw[:, c, 0:1], col(CONV_B, c),
                                     ALU.mult, ALU.add))
                for k in range(1, W):
                    link(V.scalar_tensor_tensor(acc, cprompt[:, c, k:k + SEQ], convw[:, c, k:k + 1], acc,
                                                ALU.mult, ALU.add))
                dve.wait_ge(prod_ready, DS * (c + 1))
                tail = conv[:, c, SEQ:T]
                V.tensor_reduce(tail, prod[:].rearrange("p b t k -> p (b t) k"), AX.X, ALU.add
                                ).then_inc(prod_used, 1)
                dve.wait_ge(prod_used, c + 1)
                V.tensor_scalar(tail, tail, col(CONV_B, c), None, ALU.add).then_inc(conv_done, 1)

            for c in range(2):
                glu(c)
            convolve(0)
            for c in range(2, KC):
                glu(c)
                if c % 2:
                    convolve(c // 2)
            for c in range(KC // 2, KC):
                convolve(c)
            dve.wait_ge(v_rows, 2 * KC)
            for tt in range(NT):
                r = ROWS[tt]
                for h in range(2):
                    link(V.bn_stats(bnst[0:r, tt, h, :], stage[0:r, tt, h * 512:(h + 1) * 512]))
                ins = V.bn_aggr(mv[0:r, tt, :], bnst[0:r, tt, :, :])
                if tt < NT - 1:
                    link(ins)
            ins.then_inc(v_stats, 1)
            dve.wait_ge(mean_ready, 1)
            ins = V.tensor_tensor(conv, conv, bank[4][:, 0:T].unsqueeze(1).to_broadcast([P, KC, T]), ALU.subtract)
            ins.then_inc(centered, 1)
            dve.wait_ge(rooted, 3)
            link(V.reciprocal(ss[:, 8:10], ss[:, 8:10]))
            link(V.reciprocal(ss[0:NS, 10:11], ss[0:NS, 10:11]))
            dve.wait_ge(lnv_in, 48)
            for tt in range(NT):
                r = ROWS[tt]
                row = stage[0:r, tt, :]
                link(V.tensor_scalar(row, row, mv[0:r, tt, 0:1], ss[0:r, 8 + tt:9 + tt], ALU.subtract, ALU.mult))
                link(V.tensor_tensor(row, row, lnv_g[0:r], ALU.mult))
                V.tensor_tensor(row, row, lnv_b[0:r], ALU.add).then_inc(v_normed, 1)
            dve.wait_ge(ws_ready, 1)
            ps = bank[6][0:NS, 0:G * DS].rearrange("p (g i) -> p g i", g=G)
            for b in range(DB):
                ins = V.tensor_scalar(WS[:, :, b * DS:(b + 1) * DS], ps, bmask[:, b:b + 1], None, ALU.mult)
            ins.then_inc(ws_raw, 1)
            dve.wait_ge(rooted, 4)
            link(V.reciprocal(dev_inv, dev_inv))
            V.tensor_tensor(conv, conv, dev_inv.unsqueeze(1).to_broadcast([P, KC, T]), ALU.mult).then_inc(conv_normed, 1)
            for g in range(G):
                dve.wait_ge(sp_ready, g + 1)
                b = bank[4 + g % 4]
                sp = sq[:, g, :]
                V.tensor_tensor(sp[:, 0:SEQ].rearrange("p (c i) -> p c i", c=2),
                                b[:, 0:SEQ].rearrange("p (c i) -> p c i", c=2),
                                spb[:, g:g + 1, :].to_broadcast([P, 2, P]), ALU.add)
                V.tensor_tensor(sp[:, SEQ:T].rearrange("p (b i) -> p b i", b=DB),
                                b[:, SEQ:T].rearrange("p (b i) -> p b i", b=DB),
                                spb[:, g:g + 1, 0:DS].to_broadcast([P, DB, DS]), ALU.add).then_inc(sp_evac, 1)
                dve.wait_ge(sp_evac, 2 * g + 1)
                V.tensor_tensor(uT[:, g, :], uT[:, g, :], sp, ALU.mult).then_inc(sp_evac, 1)
            for c in range(KC):
                dve.wait_ge(yb_ready, c + 1)
                V.scalar_tensor_tensor(gbT[:, c, :], bank[c % 4][:, 0:T], col(B_B, c), gbT[:, c, :],
                                       ALU.add, ALU.mult).then_inc(yb_evac, 1)
            for c in range(KC):
                dve.wait_ge(ya_ready, c + 1)
                V.tensor_tensor(gaT[:, c, :], bank[c % 4][:, 0:T], gaT[:, c, :], ALU.mult).then_inc(ya_evac, 1)
                dve.wait_ge(ya_evac, 2 * c + 1)
                V.tensor_tensor(gaT[:, c, :], gaT[:, c, :], gbT[:, c, :], ALU.add).then_inc(ya_evac, 1)
            for c in range(KC):
                dve.wait_ge(mo_transposed, c + 1)
                b = bank[4 + c % 4]
                x01 = xt[:, 0:2, c * P:(c + 1) * P]
                V.tensor_tensor(x01, x01, b[:, 0:2 * P].rearrange("p (t d) -> p t d", t=2), ALU.add)
                x2 = xt[0:NS, 2, c * P:(c + 1) * P]
                V.tensor_tensor(x2, x2, b[0:NS, 2 * P:3 * P], ALU.add).then_inc(x2_ready, 1)
            dve.wait_ge(rooted, 5)
            link(V.reciprocal(ss[:, 4:4 + NT], ss[:, 4:4 + NT]))
            for tt in range(NT):
                V.tensor_scalar(stage[:, tt, :], xt[:, tt, :], ss[:, 4 + tt:5 + tt], None, ALU.mult
                                ).then_inc(xs2_ready, 1)
            link(V.memset(lx[:, :, NE:NE + 8], SENTINEL))
            link(V.memset(want8[:, :, TOPK:8], SENTINEL))
            link(V.memset(lx[:, 2, 0:NE], 0.0))
            dve.wait_ge(wr_in, 32)
            dve.wait_ge(logits_ready, 1)
            lps = bank[0][:, 0:NT * NE].rearrange("p (t e) -> p t e", t=NT)
            V.tensor_tensor(lx[:, 0:2, 0:NE], lps[:, 0:2], br[:].unsqueeze(1).to_broadcast([P, 2, NE]), ALU.add)
            link(V.tensor_tensor(lx[0:NS, 2, 0:NE], lps[0:NS, 2], br[0:NS, :], ALU.add))
            for tt in range(NT):
                link(V.max(top8[:, tt, :], lx[:, tt, 0:NE]))
            link(V.tensor_copy(want8[:, :, 0:TOPK], top8[:, :, 0:TOPK]))
            V.tensor_tensor(gates[:], lx[:, :, 0:NE], top8[:, :, 0:1].to_broadcast([P, NT, NE]), ALU.subtract
                            ).then_inc(shifted, 1)
            for tt in range(NT):
                link(V.match_replace(lr[:, tt, :], want8[:, tt, :], lx[:, tt, :], -SENTINEL))
            link(V.tensor_tensor(mask[:], lr[:, :, 0:NE], lx[:, :, 0:NE], ALU.not_equal))
            dve.wait_ge(exped, 1)
            link(V.tensor_tensor(gates[:], gates[:], mask[:], ALU.mult))
            link(V.tensor_reduce(ss[:, 12:12 + NT], gates[:], AX.X, ALU.add))
            link(V.reciprocal(ss[:, 12:12 + NT], ss[:, 12:12 + NT]))
            link(V.tensor_tensor(gates[:], gates[:], ss[:, 12:12 + NT].unsqueeze(2).to_broadcast([P, NT, NE]), ALU.mult))
            for lo, hi in ((NS, 64), (64, P)):
                V.memset(gates[lo:hi, 2, :], 0.0)
                link(V.memset(mask[lo:hi, 2, :], 0.0))
            V.memset(out_sb, 0.0).then_inc(out_ready, 1)
            V.memset(combT[1], 0.0).then_inc(combT_ready, 1)
            V.tensor_scalar(rankm[:], mask[:], ABSENT, -ABSENT, ALU.mult, ALU.add).then_inc(routed, 1)
            dve.wait_ge(rank_ready, 1)
            rps = bank[1][:, 0:NT * NE].rearrange("p (t e) -> p t e", t=NT)
            link(V.tensor_tensor(rankm[:], rankm[:], rps, ALU.add))
            for r in range(MAX_ROUNDS + 1):
                V.tensor_scalar(tbl_rank[:, :, r * NE:(r + 1) * NE], rankm[:], -float(BLK * r), None, ALU.add)
                link(V.tensor_copy(tbl_gate[:, :, r * NE:(r + 1) * NE], gates[:]))
            link(V.tensor_reduce(ss[:, 0:1], bank[2][:, 0:NE], AX.X, ALU.max))
            link(V.tensor_scalar(ss[:, 1:2], ss[:, 0:1], 0.0, NE / 2, ALU.is_gt, ALU.mult))
            for r in range(1, MAX_ROUNDS):
                link(V.tensor_scalar(ss[:, 2:3], ss[:, 0:1], float(BLK * r), NE / 2, ALU.is_gt, ALU.mult))
                link(V.tensor_tensor(ss[:, 1:2], ss[:, 1:2], ss[:, 2:3], ALU.add))
            V.tensor_copy(n_pairs[:], ss[:, 1:2]).then_inc(pairs_known, 1)
            for tt in range(NT):
                dve.wait_ge(bd_ready, tt + 1)
                r = ROWS[tt]
                for h in range(2):
                    dst = xt[0:r, tt, h * 512:(h + 1) * 512]
                    ins = V.tensor_tensor(dst, dst, (Y0, Y1)[h][0:r, :], ALU.add)
                ins.then_inc(y_added, 1)

            def select(i, s):
                for tt in range(NT):
                    rank = tbl_rank[:, tt, bass.ds(i, 1)]
                    V.tensor_scalar(sel[s][:, tt, :], slot_ids[:, 0, :], rank, None, ALU.is_equal)
                    ins = V.tensor_scalar(comb[s][:, tt], slot_ids[:], rank, tbl_gate[:, tt, bass.ds(i, 1)],
                                          ALU.is_equal, ALU.mult)
                ins.then_inc(sel_ready, 1)

            def take_x(s):
                V.tensor_tensor(xT[s], XB[:, :].rearrange("p (k t) -> p k t", k=KC),
                                cols[:, NORM_FFN, :].unsqueeze(2).to_broadcast([P, KC, BLK]), ALU.mult
                                ).then_inc(xT_ready, 1)

            select(0, 0)
            dve.wait_ge(gathered, 1)
            take_x(0)
            pairs = dve.value_load(n_pairs[0:1, 0:1], min_val=NE // 2, max_val=MAX_ROUNDS * NE // 2)
            base0 = link.count[0]
            with dve.Fori(0, pairs) as ip:
                n_links = [0]

                def step(ins):
                    n_links[0] += 1
                    ins.then_inc(dve_step, 1)
                    dve.wait_ge(dve_step, ip * LINKS + (base0 + n_links[0]))

                for s in range(2):
                    i = ip * 2 + s
                    used = ip * (2 * SLOTS) + s * SLOTS
                    dve.wait_ge(combT_ready, i + 1)
                    select(i + 1, 1 - s)
                    dve.wait_ge(slots_used, used + UP_SLOTS)
                    V.tensor_copy(raw_u, U1[:, :]).then_inc(raw_u_ready, 1)
                    dve.wait_ge(gathered, i + 2)
                    take_x(1 - s)
                    def bias(z, q):
                        f = (2 * z + q) * 4
                        return bupT[:, bass.ds(i & (NE - 1), 1), f:f + 4].rearrange("p e c -> p (e c)") \
                            .unsqueeze(2).to_broadcast([P, 4, BLK])

                    def shaped(t):
                        return t.rearrange("p (c q t) -> p c q t", c=4, q=2)

                    for z, (src, dst) in enumerate(((T0, g1), (T1, u1))):
                        dve.wait_ge(turned, ip * 4 + (2 * s + z + 1))
                        for q in range(2):
                            ins = V.tensor_tensor(shaped(dst)[:, :, q, :], shaped(src[:, :])[:, :, q, :],
                                                  bias(z, q), ALU.add)
                        step(ins)
                        if z == 0:
                            V.tensor_scalar(g1, g1, LIMIT, None, ALU.min).then_inc(g1_ready, 1)
                        else:
                            step(V.tensor_scalar(u1, u1, LIMIT, -LIMIT, ALU.min, ALU.max))
                    dve.wait_ge(sig_ready, i + 1)
                    step(V.tensor_tensor(gs, g1, sg, ALU.mult))
                    V.scalar_tensor_tensor(actT, u1, 1.0, gs, ALU.add, ALU.mult).then_inc(act_ready, 1)
                    add_outputs(dve, ip * (2 * NT) + NT * s)
                assert n_links[0] == LINKS
            add_outputs(dve, pairs * (2 * NT))
            dve.wait_ge(fing_in, 16)
            base1 = pairs * LINKS + base0
            dve.wait_ge(rooted, 6)
            V.reciprocal(ss[:, 4:4 + NT], ss[:, 4:4 + NT]).then_inc(dve_step, 1)
            dve.wait_ge(dve_step, base1 + 1)
            for tt in range(NT):
                r = ss[:, 4 + tt:5 + tt]
                V.scalar_tensor_tensor(xt[:, tt, :], xt[:, tt, :], r, fing, ALU.mult, ALU.mult).then_inc(y_ready, 1)

        @block.tensor
        def _(pe):
            mm = nc.tensor.matmul

            def tr(dst, src):
                n = src.shape[0]
                return nc.tensor.transpose(dst, src, ident[0:n, 0:n])

            pe.wait_ge(const_ready, 4)
            pe.wait_ge(vec_in, 16 * 8)
            tr(bank[7][:, 0:8 * KC], vecrows[:]).then_inc(pe_early, 1)
            pe.wait_ge(evac_early, 1)
            pe.wait_ge(xs_ready, NT)
            for c in range(KC):
                for tt in range(NT):
                    r = ROWS[tt]
                    ins = tr(bank[c][:, tt * P:tt * P + r], stage[0:r, tt, c * P:(c + 1) * P])
                ins.then_inc(x_transposed, 1)

            def project(n, h, dst, src):
                w = ring[:, n % SLOTS, :].rearrange("p (k n) -> p k n", k=KC)
                if h == 0:
                    pe.wait_ge(slot_full[n % SLOTS], 16 * (n // SLOTS + 1))
                for k in range(KC):
                    ins = mm(dst[:, 0:T], w[:, k, h * P:(h + 1) * P], src[:, k, :], start=k == 0, stop=k == KC - 1)
                return ins

            pe.wait_ge(hT_ready, KC)
            for j in range(KC // 2):
                if j >= 2:
                    pe.wait_ge(glu_ready, 2 * (j - 1))
                for part in range(2):
                    n = 2 * j + part
                    for h in range(2):
                        project(n, h, bank[4 * (j % 2) + 2 * part + h], hT[:]).then_inc(c_proj, 1)
                if j == 0:
                    pe.wait_ge(cache_in, 32)
                    for c in range(KC):
                        for h in range(2):
                            lo = ((c % 2) * 2 + h) * 4 * HIST
                            ins = tr(bank[4 + c // 2][:, lo:lo + 4 * HIST], cache_rows[:, h, c * P:(c + 1) * P])
                    ins.then_inc(pe_early, 1)
                    pe.wait_ge(evac_early, 2)
                    pe.wait_ge(cw_in, 16)
                    for c in range(KC):
                        ins = tr(bank[4][:, c * W:(c + 1) * W], cw_rows[:, c * P:(c + 1) * P])
                    ins.then_inc(pe_early, 1)
                    pe.wait_ge(bup_in, 16)
                    for f in range(2 * KC):
                        ins = tr(bank[5][:, f * NE:(f + 1) * NE], bup_rows[:, f * P:(f + 1) * P])
                    ins.then_inc(pe_early, 1)
                    pe.wait_ge(wsp_in, 16)
                    for g in range(G):
                        ins = tr(bank[6 + g // 4][:, (g % 4) * P:(g % 4 + 1) * P], wsp[:, g, :])
                    ins.then_inc(pe_early, 1)
                    pe.wait_ge(evac_early, 5)
            pe.wait_ge(glu_ready, KC)
            for n in range(4 * KC):
                kind, c = divmod(n, KC)
                if n >= 4:
                    pe.wait_ge(act_evac, n - 3)
                project(8 + n // 2, n % 2, bank[n % 4], hT[:]).then_inc(proj, 1)
                if 1 <= n <= KC:
                    turn_v(pe, tr, n - 1)
                if n == KC:
                    pe.wait_ge(tail_packed, 1)
                    for q in range(2):
                        for c2 in range(KC):
                            if c2 == 4:
                                pe.wait_ge(st_ready, 1) if q == 0 else pe.wait_ge(st_ready, 3)
                            dst = bank[6 + q][0:(HIST, NS)[q], (c2 % 4) * P:(c2 % 4 + 1) * P]
                            src = cprompt[:, c2, SEQ:SEQ + HIST] if q == 0 else glu_tail[:, c2, :]
                            nc.tensor.transpose(dst, src, ident[:]).then_inc(st_transposed, 1)
                if n == 2 * KC - 1:
                    pe.wait_ge(conv_done, KC)
                    pe.wait_ge(v_rows, 2 * KC)
                    for c2 in range(KC):
                        ins = mm(bank[4][:, 0:T], mean_w[:], conv[:, c2, :], start=c2 == 0, stop=c2 == KC - 1)
                    ins.then_inc(mean_ready, 1)
                    pe.wait_ge(wt_masked, 1)
                    pe.wait_ge(ws_raw, 1)
                    pe.wait_ge(st_ready, 4)
                    mm(bank[6][0:NS, 0:G * DS].rearrange("p (g i) -> p g i", g=G), rep4[:].rearrange("p b j -> p (b j)"),
                       WT[0:DS, :, 0:DS], start=True, stop=True).then_inc(ws_ready, 1)
                if n == 3 * KC - 1:
                    pe.wait_ge(sq_ready, 1)
                    for c2 in range(KC):
                        ins = mm(bank[5][:, 0:T], mean_w[:], sq[:, c2, :], start=c2 == 0, stop=c2 == KC - 1)
                    ins.then_inc(var_ready, 1)
            pe.wait_ge(v_normed, NT)
            pe.wait_ge(ws_raw, 2)
            pe.wait_ge(conv_normed, 1)
            for g in range(G):
                if g >= 4:
                    pe.wait_ge(sp_evac, 2 * (g - 4) + 1)
                b = bank[4 + g % 4]
                for c in range(2):
                    mm(b[:, c * P:(c + 1) * P], stage[:, c, g * P:(g + 1) * P], WT[:, g, :], start=True, stop=True)
                mm(b[:, SEQ:T], stage[0:NS, 2, g * P:(g + 1) * P], WS[:, g, :], start=True, stop=True
                   ).then_inc(sp_ready, 1)
            for m in range(KC):
                if m == 0:
                    pe.wait_ge(silu_done, KC)
                if m < 4:
                    pe.wait_ge(act_evac, 4 * KC - 3 + m)
                else:
                    pe.wait_ge(yb_evac, m - 3)
                project(24 + m // 2, m % 2, bank[m % 4], conv).then_inc(yb_ready, 1)
            for m in range(KC):
                if m == 0:
                    pe.wait_ge(sp_evac, 2 * G)
                if m < 4:
                    pe.wait_ge(yb_evac, KC - 3 + m)
                else:
                    pe.wait_ge(ya_evac, 2 * (m - 4) + 1)
                project(28 + m // 2, m % 2, bank[m % 4], uT).then_inc(ya_ready, 1)
            for m in range(KC):
                if m == 0:
                    pe.wait_ge(ya_evac, 2 * KC)
                if m >= 4:
                    pe.wait_ge(mo_evac, m - 3)
                project(32 + m // 2, m % 2, bank[m % 4], gaT).then_inc(mo_ready, 1)
                if m >= 1:
                    turn_mixed(pe, tr, m - 1)
            turn_mixed(pe, tr, KC - 1)
            pe.wait_ge(xs2_ready, NT)
            pe.wait_ge(mo_evac, KC)
            for c in range(KC):
                for tt in range(NT):
                    r = ROWS[tt]
                    ins = tr(bank[c][:, tt * P:tt * P + r], stage[0:r, tt, c * P:(c + 1) * P])
                ins.then_inc(x2_transposed, 1)
            pe.wait_ge(h2T_ready, KC)
            pe.wait_ge(wr_in, 32)
            for tt in range(NT):
                for k in range(KC):
                    ins = mm(bank[0][0:ROWS[tt], tt * NE:(tt + 1) * NE], hT[:, k, token_slices(tt)], wr[:, k, :],
                             start=k == 0, stop=k == KC - 1)
            ins.then_inc(logits_ready, 1)
            pe.wait_ge(routed, 1)
            for tt in range(NT):
                for t2 in range(tt + 1):
                    ins = mm(bank[1][:, tt * NE:(tt + 1) * NE], (below if t2 == tt else ones)[:], mask[:, t2, :],
                             start=t2 == 0, stop=t2 == tt)
            for t2 in range(NT):
                ins = mm(bank[2][:, 0:NE], ones[:], mask[:, t2, :], start=t2 == 0, stop=t2 == NT - 1)
            ins.then_inc(rank_ready, 1)
            for tt in range(NT):
                r = ROWS[tt]
                ins = tr(bank[5][0:NE, tt * P:tt * P + r], gates[0:r, tt, :])
            ins.then_inc(gT_ready, 1)
            pe.wait_ge(gT_evac, 1)
            pe.wait_ge(bdown_in, 16)
            for tt in range(NT):
                if tt:
                    pe.wait_ge(y_added, tt)
                for h in range(2):
                    ins = mm((Y0, Y1)[h][0:ROWS[tt], :], gateT[:, token_slices(tt)], bdown[:, h * 512:(h + 1) * 512],
                             start=True, stop=True)
                ins.then_inc(bd_ready, 1)

            def gather(s):
                for k in range(KC):
                    for tt in range(NT):
                        ins = mm(XB[:, k * BLK:(k + 1) * BLK], stage[:, tt, k * P:(k + 1) * P], sel[s][:, tt, :],
                                 start=tt == 0, stop=tt == NT - 1)
                ins.then_inc(gathered, 1)

            def combine(s, tt):
                for q in range(2):
                    dst = row_banks[tt][q]
                    ins = mm(dst[:, :], combT[s][q * BLK:(q + 1) * BLK, tt * P:(tt + 1) * P],
                             out_sb[q * BLK:(q + 1) * BLK, :], start=True, stop=True)
                ins.then_inc(combined, 1)

            pe.wait_ge(sel_ready, 1)
            gather(0)
            pe.wait_ge(pairs_known, 1)
            pairs = pe.value_load(n_pairs[0:1, 0:1], min_val=NE // 2, max_val=MAX_ROUNDS * NE // 2)
            with pe.Fori(0, pairs) as ip:
                for s in range(2):
                    i = ip * 2 + s
                    fills = ip * 32 + 16 * (FILLS + 1 + s)
                    pe.wait_ge(xT_ready, i + 1)
                    pe.wait_ge(y_added, ip * (2 * NT) + (NT * s + 2))
                    for k in range(UP_SLOTS):
                        pe.wait_ge(slot_full[k], fills)
                        for z, dst in enumerate((U0, U1)):
                            for q in range(2):
                                lo = z * D + q * 512
                                ins = mm(dst[q * BLK:(q + 1) * BLK, :], xT[s][:, k, :], ring[:, k, lo:lo + 512],
                                         start=k == 0, stop=k == UP_SLOTS - 1)
                        ins.then_inc(slots_used, 1)
                    pe.wait_ge(sel_ready, i + 2)
                    pe.wait_ge(combT_ready, i + 1)
                    gather(1 - s)
                    for z, (src, dst, ready) in enumerate(((raw_g, T0, raw_g_ready), (raw_u, T1, raw_u_ready))):
                        pe.wait_ge(ready, i + 1)
                        for c in range(4):
                            ins = tr(dst[:, c * P:(c + 1) * P], src[:, c * P:(c + 1) * P])
                        ins.then_inc(turned, 1)
                    pe.wait_ge(out_ready, i + 1)
                    pe.wait_ge(y_added, ip * (2 * NT) + (NT * s + NT))
                    combine(1 - s, 0)
                    combine(1 - s, 1)
                    pe.wait_ge(xT_ready, i + 2)
                    for tt in range(NT):
                        ins = tr(XB[:, tt * P:(tt + 1) * P], comb[s][:, tt].rearrange("p q j -> p (q j)"))
                    ins.then_inc(combT_turned, 1)
                    pe.wait_ge(y_added, ip * (2 * NT) + (NT * s + NT + 1))
                    combine(1 - s, 2)
                    pe.wait_ge(act_ready, i + 1)
                    for j in range(SLOTS - UP_SLOTS):
                        k = UP_SLOTS + j
                        pe.wait_ge(slot_full[k], fills)
                        for h in range(2):
                            f = 2 * j + h
                            lhsT = actT.rearrange("p (c q t) -> p c q t", c=4, q=2)[:, f % 4, f // 4, :]
                            for q in range(2):
                                lo = h * D + q * 512
                                ins = mm(DN[q * BLK:(q + 1) * BLK, :], lhsT, ring[:, k, lo:lo + 512],
                                         start=f == 0, stop=f == KC - 1)
                        ins.then_inc(slots_used, 1)
            pe.wait_ge(out_ready, pairs * 2 + 1)
            pe.wait_ge(y_added, pairs * (2 * NT) + NT)
            for tt in range(NT):
                if tt == 2:
                    pe.wait_ge(y_added, pairs * (2 * NT) + (NT + 1))
                combine(1, tt)



INPUTS = ["x_prompt", "x_sample", "cache_conv", "norm_mix_g", "w_in", "ln_v_g", "ln_v_b", "w_spatial", "b_spatial",
          "w_branch_a", "conv_w", "conv_b", "ln_conv_g", "ln_conv_b", "w_branch_b", "b_branch_b", "b_gate_a",
          "b_gate_b", "w_out", "norm_ffn_g", "w_router", "b_router", "w_up", "b_up", "w_down", "b_down",
          "norm_final_g"]
OUTPUTS = {"y_prompt": (1, SEQ, D), "y_sample": (DB, DS, D), "conv_state_prompt": (1, 1, HIST, D),
           "conv_state_sample": (1, DB, HIST, D), "chunk_v_sample": (1, DB, DS, D)}


def kernel(**inputs):
    import numpy as np
    import concourse.bacc as bacc
    from concourse.bass_utils import run_bass_kernel_spmd

    nc = bacc.Bacc("TRN2", target_bir_lowering=False, num_devices=1)
    arrays, a, out = {}, {}, {}
    for name in INPUTS:
        x = np.ascontiguousarray(inputs[name])
        arrays[f"in_{name}"] = x
        a[name] = nc.dram_tensor(f"in_{name}", x.shape, F32, kind="ExternalInput").ap()
    for name, shape in OUTPUTS.items():
        out[name] = nc.dram_tensor(f"out_{name}", shape, F32, kind="ExternalOutput").ap()
    hybrid_layer(nc, a, out)
    result = run_bass_kernel_spmd(nc, [arrays], core_ids=[0]).results[0]
    return tuple(result[f"out_{name}"] for name in OUTPUTS)
```

```python
import concourse.bass as bass
from concourse import mybir
from contextlib import ExitStack

F32 = mybir.dt.float32
I32 = mybir.dt.int32
ALU = mybir.AluOpType
ACT = mybir.ActivationFunctionType
AX = mybir.AxisListType

P = 128
D = 1024
KC = D // P
SEQ = 256
DB, DS = 8, 4
NS = DB * DS
T = SEQ + NS
NT = 3
ROWS = [P, P, NS]
W = 31
HIST = W - 1
SEG = HIST + DS
CB = HIST + SEQ + DB * SEG
G = 8
NE = 32
TOPK = 4
BLK = 64
MAX_ROUNDS = -(-T // BLK)
TBL = MAX_ROUNDS * NE
MAX_ITEMS = NE + (T * TOPK) // BLK
SLOTS = 12
SLOT = 2048
UP_SLOTS = 8
MIX_BLOCKS = 36
FILLS = MIX_BLOCKS // SLOTS
EPS = 1e-5
LIMIT = 7.0
ALPHA = 1.702
ABSENT = 4096.0
SENTINEL = 3.0e38


def token_slices(tt):
    return slice(tt * P, tt * P + ROWS[tt])


def mix_block_source(n, w_in, w_a, w_b, w_out):
    c0 = 2 * D
    if n < 8:
        start = c0 + (n % 2) * D + (n // 2) * 256
        src = w_in[0, :, start:start + 256]
    elif n < 24:
        base = [D, 0, 4 * D, 5 * D][(n - 8) // 4]
        start = base + (n % 4) * 256
        src = w_in[0, :, start:start + 256]
    else:
        w = [w_b, w_a, w_out][(n - 24) // 4]
        src = w[0, :, (n % 4) * 256:(n % 4) * 256 + 256]
    return src.rearrange("(k p) n -> p k n", p=P)


def hybrid_layer(nc, a, out):
    with ExitStack() as ctx:
        def sb(name, shape, dt=F32):
            return ctx.enter_context(nc.sbuf_tensor(name, shape, dt))

        def sem(name):
            return ctx.enter_context(nc.semaphore(name))

        ring = sb("ring", [P, SLOTS, SLOT])
        xt = sb("xt", [P, NT, D])
        stage = sb("stage", [P, NT, D])
        hT = sb("hT", [P, KC, T])
        ident = sb("ident", [P, P])
        mean_w = sb("mean_w", [P, P])
        ones = sb("ones", [P, P])
        below = sb("below", [P, P])
        slot_ids = sb("slot_ids", [P, 2, BLK])
        cols = sb("cols", [P, 8, KC])
        convw = sb("convw", [P, KC, W])
        vecrows = sb("vecrows", [BLK, P])
        bupT = sb("bupT", [P, NE, 2 * KC])
        wr = sb("wr", [P, KC, NE])
        br = sb("br", [P, NE])
        spb = sb("spb", [P, G, P])
        WT = sb("WT", [P, G, P])
        WS = sb("WS", [NS, G, NS])
        bmask = sb("bmask", [NS, DB])
        rep4 = sb("rep4", [DS, DB, DS])
        tmpc = sb("tmpc", [P, 2, T])
        tmpv = stage[:, 0, 0:2 * T].rearrange("p (h t) -> p h t", h=2)
        eps_col = sb("eps_col", [P, 1])
        glu_tail = sb("glu_tail", [P, KC, NS])
        ss = sb("ss", [P, 16])
        bnst = sb("bnst", [P, NT, 2, 6])
        mv = sb("mv", [P, NT, 2])
        n_items = sb("n_items", [P, 1], I32)
        items = sb("items", [1, P], I32)
        item_ids = sb("item_ids", [P, 2])
        big = sb("big", [P, KC * CB])
        R1 = sb("R1", [P, KC * T])
        R2 = sb("R2", [P, KC * T])
        R3 = sb("R3", [P, KC * T])
        R4 = sb("R4", [P, KC * T])

        def view(t, c):
            return t[:, :].rearrange("p (c t) -> p c t", c=c)

        convbuf = view(big, KC)
        cprompt = convbuf[:, :, 0:HIST + SEQ]
        csample = convbuf[:, :, HIST + SEQ:CB].rearrange("p c (b s) -> p c b s", b=DB)
        conv = view(R1, KC)
        uT = view(R2, KC)
        gaT = view(R3, KC)
        gbT = view(R4, KC)
        sq = big[:, 0:KC * T].rearrange("p (c t) -> p c t", c=KC)
        bup_rows = R1[0:NE, 0:2 * D]
        wsp = R2[:, 0:G * P].rearrange("p (g j) -> p g j", g=G)
        cw_rows = R2[0:W, G * P:G * P + D]
        cache_rows = R3[0:4 * HIST, 0:2 * D].rearrange("p (h c) -> p h c", h=2)
        lnv_g = R4[:, 0:D]
        lnv_b = R4[:, D:2 * D]
        st_rows = R3[0:NS, 0:2 * D].rearrange("p (q c) -> p q c", q=2)
        prod = sb("prod", [P, DB, DS, W])

        pos = {"big": 0, "R1": 0, "R2": 0, "R4": 0}
        regs = {"big": big, "R1": R1, "R2": R2, "R4": R4}

        def carve(region, n, rows=P):
            lo = pos[region]
            pos[region] = lo + n
            assert pos[region] <= regs[region].shape[1]
            return regs[region][0:rows, lo:lo + n]

        xT = carve("big", KC * BLK).rearrange("p (k t) -> p k t", k=KC)
        raw_g, raw_u = carve("big", 512), carve("big", 512)
        g1, sg, u1, gs = (carve("big", 512) for _ in range(4))
        actT = carve("R1", 512)
        out_sb = carve("R1", 512)
        sel = carve("R1", NT * BLK).rearrange("p (t j) -> p t j", t=NT)
        comb = carve("R1", NT * P).rearrange("p (t q j) -> p t q j", t=NT, q=2)
        lg = carve("R1", NT * NE).rearrange("p (t e) -> p t e", t=NT)
        combT = carve("R2", NT * P)
        tbl_rank = carve("R2", NT * TBL).rearrange("p (t i) -> p t i", t=NT)
        tbl_gate = carve("R2", NT * TBL).rearrange("p (t i) -> p t i", t=NT)
        gateT = carve("R4", T, NE)
        bdown = carve("R4", D, NE)
        lx = carve("R4", NT * (NE + 8)).rearrange("p (t e) -> p t e", t=NT)
        lr = carve("R4", NT * (NE + 8)).rearrange("p (t e) -> p t e", t=NT)
        top8 = carve("R4", NT * 8).rearrange("p (t e) -> p t e", t=NT)
        want8 = carve("R4", NT * 8).rearrange("p (t e) -> p t e", t=NT)
        mask = carve("R4", NT * NE).rearrange("p (t e) -> p t e", t=NT)
        gates = carve("R4", NT * NE).rearrange("p (t e) -> p t e", t=NT)
        rankm = carve("R4", NT * NE).rearrange("p (t e) -> p t e", t=NT)
        def extra_table():
            return carve("big", (MAX_ROUNDS - 1) * NE).rearrange("p (r e) -> p r e", e=NE)

        need, pos_a, pos_b, col_ids = (extra_table() for _ in range(4))
        item_row = carve("R1", 1)
        fing = R3[:, 0:D]

        bank = [ctx.enter_context(nc.psum_tensor(f"bank{i}", [P, 512], F32)) for i in range(8)]
        U0, U1, T0, T1, XB, DN, Y0, Y1 = bank

        slot_full = [sem(f"slot_full{k}") for k in range(SLOTS)]
        vec_in, cw_in, cache_in, wsp_in, bup_in, lnv_in, wr_in = (
            sem(n) for n in ("vec_in", "cw_in", "cache_in", "wsp_in", "bup_in", "lnv_in", "wr_in"))
        x_in = [sem(f"x_in{tt}") for tt in range(NT)]
        bdown_in, fing_in = sem("bdown_in"), sem("fing_in")
        stored, v_stored, st_stored = sem("stored"), sem("v_stored"), sem("st_stored")
        old_rows_stored = sem("old_rows_stored")
        slots_used = sem("slots_used")
        const_step, const_ready = sem("const_step"), sem("const_ready")
        pads_zero, history_zero = sem("pads_zero"), sem("history_zero")
        pe_early, evac_early = sem("pe_early"), sem("evac_early")
        ws_raw, ws_ready, wt_masked = sem("ws_raw"), sem("ws_ready"), sem("wt_masked")
        squared, xs_ready = sem("squared"), sem("xs_ready")
        x_transposed, hT_ready = sem("x_transposed"), sem("hT_ready")
        c_proj, gate_sig, glu_ready = sem("c_proj"), sem("gate_sig"), sem("glu_ready")
        proj, act_evac = sem("proj"), sem("act_evac")
        v_transposed, v_rows = sem("v_transposed"), sem("v_rows")
        tail_packed = sem("tail_packed")
        st_transposed, st_ready = sem("st_transposed"), sem("st_ready")
        prod_ready, prod_used = sem("prod_ready"), sem("prod_used")
        conv_done, mean_ready, sq_ready, var_ready, conv_normed, silu_done = (
            sem(n) for n in ("conv_done", "mean_ready", "sq_ready", "var_ready", "conv_normed", "silu_done"))
        centered = sem("centered")
        v_normed = sem("v_normed")
        sp_ready, sp_evac = sem("sp_ready"), sem("sp_evac")
        yb_ready, yb_evac = sem("yb_ready"), sem("yb_evac")
        ya_ready, ya_evac = sem("ya_ready"), sem("ya_evac")
        mo_ready, mo_evac = sem("mo_ready"), sem("mo_evac")
        mo_transposed, x2_ready = sem("mo_transposed"), sem("x2_ready")
        v_stats, rooted = sem("v_stats"), sem("rooted")
        sums_added = sem("sums_added")
        squared2, xs2_ready, x2_transposed, h2T_ready = (
            sem(n) for n in ("squared2", "xs2_ready", "x2_transposed", "h2T_ready"))
        col_ids_ready, listed, list_turned = sem("col_ids_ready"), sem("listed"), sem("list_turned")
        logits_ready, shifted, exped, routed = (
            sem(n) for n in ("logits_ready", "shifted", "exped", "routed"))
        rank_ready, gT_ready, gT_evac, bd_ready, items_known = (
            sem(n) for n in ("rank_ready", "gT_ready", "gT_evac", "bd_ready", "items_known"))
        comb_ready, turned_read = sem("comb_ready"), sem("turned_read")
        sel_ready, gathered, xT_ready = sem("sel_ready"), sem("gathered"), sem("xT_ready")
        raw_g_ready, raw_u_ready, turned = sem("raw_g_ready"), sem("raw_u_ready"), sem("turned")
        g1_ready, sig_ready, act_ready = sem("g1_ready"), sem("sig_ready"), sem("act_ready")
        combT_turned, combT_ready = sem("combT_turned"), sem("combT_ready")
        out_ready, combined, y_added = sem("out_ready"), sem("combined"), sem("y_added")
        squared3, y_ready = sem("squared3"), sem("y_ready")
        dve_step, act_step = sem("dve_step"), sem("act_step")

        NORM_MIX, GATE_A, GATE_B, B_B, CONV_B, LNC_G, LNC_B, NORM_FFN = range(8)
        vec_names = ["norm_mix_g", "b_gate_a", "b_gate_b", "b_branch_b", "conv_b", "ln_conv_g",
                     "ln_conv_b", "norm_ffn_g"]

        def col(v, c):
            return cols[:, v, c:c + 1]

        def make_link(eng, s):
            n = [0]

            def link(ins, base=None):
                n[0] += 1
                ins.then_inc(s, 1)
                eng.wait_ge(s, n[0] if base is None else base + n[0])
            link.count = n
            return link

        def mix_block_used(n):
            if n < 8:
                return c_proj, 2 * n + 2
            if n < 24:
                return proj, 2 * (n - 8) + 2
            return (yb_ready, ya_ready, mo_ready)[(n - 24) // 4], 2 * (n % 4) + 2

        LINKS = 3
        dev_inv = prod[:].rearrange("p b t k -> p (b t k)")[:, 0:T]
        row_banks = ((Y0, Y1), (U0, U1), (T0, T1))

        bias_banks = ((Y0, Y1), (U0, DN), (Y0, Y1))

        def add_bias_rows(dve, tt):
            dve.wait_ge(bd_ready, tt + 1)
            r = ROWS[tt]
            for h in range(2):
                dst = xt[0:r, tt, h * 512:(h + 1) * 512]
                ins = nc.vector.tensor_tensor(dst, dst, bias_banks[tt][h][0:r, :], ALU.add)
            ins.then_inc(y_added, 1)

        def root(dst, src, scale):
            nc.scalar.activation(dst, src, ACT.Sqrt, bias=eps_col[0:src.shape[0], :], scale=scale
                                 ).then_inc(rooted, 1)

        def load_root_table():
            nc.scalar.activation(ss[:, 15:16], eps_col[:], ACT.Sqrt, bias=eps_col[:], scale=1.0)

        def copy_v(act, c):
            b = bank[4 + c % 2]
            act.wait_ge(v_transposed, c + 1)
            nc.scalar.copy(stage[:, 0:2, c * P:(c + 1) * P], b[:, 0:2 * P].rearrange("p (t d) -> p t d", t=2)
                           ).then_inc(v_rows, 1)
            nc.scalar.copy(stage[0:NS, 2, c * P:(c + 1) * P], b[0:NS, 2 * P:3 * P]).then_inc(v_rows, 1)

        def add_outputs(dve, done):
            for tt in range(NT):
                r = ROWS[tt]
                dve.wait_ge(combined, done + (tt + 1))
                for h in range(2):
                    dst = xt[0:r, tt, h * 512:(h + 1) * 512]
                    ins = nc.vector.tensor_tensor(dst, dst, row_banks[tt][h][0:r, :], ALU.add)
                ins.then_inc(y_added, 1)

        def turn_v(pe, tr, c):
            pe.wait_ge(act_evac, c + 1)
            if c >= 2:
                pe.wait_ge(v_rows, 2 * (c - 1))
            for tt in range(NT):
                ins = tr(bank[4 + c % 2][0:ROWS[tt], tt * P:(tt + 1) * P], tmpc[:, c % 2, token_slices(tt)])
            ins.then_inc(v_transposed, 1)

        def turn_mixed(pe, tr, c):
            pe.wait_ge(mo_evac, c + 1)
            if c >= 4:
                pe.wait_ge(x2_ready, c - 3)
            for tt in range(NT):
                ins = tr(bank[4 + c % 4][0:ROWS[tt], tt * P:(tt + 1) * P], tmpc[:, c % 2, token_slices(tt)])
            ins.then_inc(mo_transposed, 1)

        block = ctx.enter_context(nc.Block())

        @block.sync
        def _(sp):
            def load(dst, src, done):
                sp.dma_start(dst, src).then_inc(done, 16)

            def load_block(n):
                if n >= SLOTS:
                    sp.wait_ge(*mix_block_used(n - SLOTS))
                load(ring[:, n % SLOTS, :].rearrange("p (k n) -> p k n", k=KC),
                     mix_block_source(n, a["w_in"], a["w_branch_a"], a["w_branch_b"], a["w_out"]),
                     slot_full[n % SLOTS])

            for tt in range(2):
                load(xt[:, tt, :], a["x_prompt"][0, tt * P:(tt + 1) * P, :], x_in[tt])
            load(xt[0:NS, 2, :], a["x_sample"].rearrange("b t d -> (b t) d"), x_in[2])
            for v, name in enumerate(vec_names):
                load(vecrows[v * KC:(v + 1) * KC, :], a[name][0].rearrange("(c p) -> c p", p=P), vec_in)
            for n in range(4):
                load_block(n)
            cache = a["cache_conv"][0].rearrange("b h c -> (b h) c")
            for h in range(2):
                load(cache_rows[:, h, :], cache[h * 4 * HIST:(h + 1) * 4 * HIST, :], cache_in)
            load(cw_rows, a["conv_w"][0], cw_in)
            load(bup_rows, a["b_up"][0], bup_in)
            load(wsp, a["w_spatial"][0].rearrange("g i j -> i g j"), wsp_in)
            for n in range(4, 8):
                load_block(n)
            load(lnv_g, a["ln_v_g"].to_broadcast([P, D]), lnv_in)
            load(lnv_b, a["ln_v_b"].to_broadcast([P, D]), lnv_in)
            load(spb[:].rearrange("p g i -> p (g i)"),
                 a["b_spatial"].rearrange("l g i -> l (g i)").to_broadcast([P, D]), lnv_in)
            load(wr[:], a["w_router"][0].rearrange("(k p) e -> p k e", p=P), wr_in)
            load(br[:], a["b_router"].to_broadcast([P, NE]), wr_in)
            for n in range(8, MIX_BLOCKS):
                load_block(n)

            def load_expert(e, used):
                for k in range(SLOTS):
                    if used is None:
                        sp.wait_ge(*mix_block_used(MIX_BLOCKS - SLOTS + k))
                    else:
                        sp.wait_ge(slots_used, used + k)
                    if k < UP_SLOTS:
                        src = a["w_up"][0, bass.ds(e, 1), k * P:(k + 1) * P, :].rearrange("e p n -> (e p) n")
                        dst = ring[:, k, :]
                    else:
                        j = k - UP_SLOTS
                        src = a["w_down"][0, bass.ds(e, 1), j * 256:(j + 1) * 256, :].rearrange(
                            "e (h p) n -> p (e h) n", p=P)
                        dst = ring[:, k, :].rearrange("p (h n) -> p h n", h=2)
                    sp.dma_start(dst, src).then_inc(slot_full[k], 16)

            load_expert(0, None)
            load_expert(1, 1)
            sp.wait_ge(items_known, 1)
            count = sp.value_load(n_items[0:1, 0:1], min_val=NE, max_val=MAX_ITEMS)
            expert_reg = sp.alloc_register("expert")
            with sp.Fori(2, count) as i:
                column = sp.value_load(items[0:1, bass.ds(i, 1)], min_val=0, max_val=TBL - 1)
                sp.reg_alu(expert_reg, column, NE - 1, ALU.bitwise_and)
                load_expert(sp.snap(expert_reg, min_val=0, max_val=NE - 1), i * SLOTS - (SLOTS - 1))
            for tt in range(NT):
                sp.wait_ge(y_ready, tt + 1)
                dst = out["y_sample"].rearrange("b t d -> (b t) d") if tt == 2 else \
                    out["y_prompt"][0, tt * P:(tt + 1) * P, :]
                sp.dma_start(dst, xt[0:ROWS[tt], tt, :]).then_inc(stored, 16)
            sp.wait_ge(stored, 16 * NT)
            sp.wait_ge(old_rows_stored, 16)
            sp.wait_ge(v_stored, 16)
            sp.wait_ge(st_stored, 16 * (1 + DB))

        @block.gpsimd
        def _(pool):
            nc.gpsimd.memset(cprompt[:, :, 0:HIST], 0.0).then_inc(history_zero, 1)
            nc.gpsimd.memset(ident[:], 0.0).then_inc(const_step, 1)
            nc.gpsimd.memset(ones[:], 1.0).then_inc(const_step, 1)
            nc.gpsimd.memset(below[:], 1.0).then_inc(const_step, 1)
            nc.gpsimd.memset(mean_w[:], 1.0 / D).then_inc(const_step, 1)
            nc.gpsimd.memset(bmask[:], 1.0).then_inc(const_step, 1)
            nc.gpsimd.memset(eps_col[:], EPS).then_inc(const_ready, 1)
            nc.gpsimd.iota(slot_ids[:], [[0, 2], [1, BLK]], base=0, channel_multiplier=0,
                           allow_small_or_imprecise_dtypes=True).then_inc(const_step, 1)
            nc.gpsimd.iota(item_ids[:], [[0, 2]], base=0, channel_multiplier=1,
                           allow_small_or_imprecise_dtypes=True).then_inc(const_step, 1)
            pool.wait_ge(const_step, 7)
            nc.gpsimd.affine_select(out=item_ids[:, 1:2], in_=item_ids[:, 1:2], compare_op=ALU.is_gt, fill=0.0,
                                    base=NE, pattern=[[0, 1]], channel_multiplier=-1).then_inc(const_ready, 1)
            nc.gpsimd.affine_select(out=ident[:], in_=ident[:], compare_op=ALU.not_equal, fill=1.0, base=0,
                                    pattern=[[-1, P]], channel_multiplier=1).then_inc(const_ready, 1)
            nc.gpsimd.affine_select(out=below[:], in_=below[:], compare_op=ALU.is_gt, fill=0.0, base=0,
                                    pattern=[[1, P]], channel_multiplier=-1).then_inc(const_ready, 1)
            nc.gpsimd.affine_select(out=bmask[:], in_=bmask[:], compare_op=ALU.is_ge, fill=0.0, base=0,
                                    pattern=[[-DS, DB]], channel_multiplier=1).then_inc(const_step, 1)
            pool.wait_ge(const_step, 8)
            nc.gpsimd.affine_select(out=bmask[:], in_=bmask[:], compare_op=ALU.is_ge, fill=0.0, base=DS - 1,
                                    pattern=[[DS, DB]], channel_multiplier=-1).then_inc(const_ready, 1)
            for_rows = a["cache_conv"][0, :, DS:HIST, :]
            pool.dma_start(out["conv_state_sample"][0, :, 0:HIST - DS, :], for_rows
                           ).then_inc(old_rows_stored, 16)
            pool.wait_ge(evac_early, 5)
            for c in range(KC):
                pool.wait_ge(gate_sig, c + 1)
                nc.gpsimd.tensor_tensor(cprompt[:, c, HIST:HIST + SEQ], tmpv[:, c % 2, 0:SEQ],
                                        tmpc[:, c % 2, 0:SEQ], ALU.mult)
                nc.gpsimd.tensor_tensor(csample[:, c, :, HIST:SEG],
                                        tmpv[:, c % 2, SEQ:T].rearrange("p (b t) -> p b t", b=DB),
                                        tmpc[:, c % 2, SEQ:T].rearrange("p (b t) -> p b t", b=DB), ALU.mult
                                        ).then_inc(glu_ready, 1)
            pool.wait_ge(glu_ready, KC)
            nc.gpsimd.tensor_copy(glu_tail[:].rearrange("p c (b t) -> p c b t", b=DB),
                                  csample[:, :, :, HIST:SEG]).then_inc(tail_packed, 1)
            nc.gpsimd.affine_select(out=WT[:], in_=WT[:], compare_op=ALU.is_ge, fill=0.0, base=0,
                                    pattern=[[0, G], [1, P]], channel_multiplier=-1).then_inc(wt_masked, 1)
            for c in range(KC):
                if c >= 1:
                    pool.wait_ge(prod_used, c)
                for t in range(DS):
                    nc.gpsimd.tensor_tensor(prod[:, :, t, :], csample[:, c, :, t:t + W],
                                            convw[:, c:c + 1, :].to_broadcast([P, DB, W]), ALU.mult
                                            ).then_inc(prod_ready, 1)
            pool.wait_ge(sp_evac, 2 * G)
            nc.gpsimd.iota(col_ids, [[1, (MAX_ROUNDS - 1) * NE]], base=NE, channel_multiplier=0,
                           allow_small_or_imprecise_dtypes=True).then_inc(col_ids_ready, 1)

        @block.scalar
        def _(act):
            act.wait_ge(pads_zero, 2)
            for tt in range(NT):
                act.wait_ge(x_in[tt], 16)
                nc.scalar.activation(stage[:, tt, :], xt[:, tt, :], ACT.Square, accum_out=ss[:, tt:tt + 1]
                                     ).then_inc(squared, 1)
            act.wait_ge(const_ready, 5)
            act.wait_ge(squared, NT)
            root(ss[:, 4:4 + NT], ss[:, 0:NT], 1.0 / D)
            act.wait_ge(evac_early, 1)
            for c in range(KC):
                act.wait_ge(x_transposed, c + 1)
                nc.scalar.mul(hT[:, c, :], bank[c][:, 0:T], col(NORM_MIX, c)).then_inc(hT_ready, 1)
            for c in range(KC):
                act.wait_ge(c_proj, 4 * (c // 2) + 3 + c % 2)
                if c >= 2:
                    act.wait_ge(glu_ready, c - 1)
                nc.scalar.activation(tmpc[:, c % 2, :], bank[4 * (c // 2 % 2) + 2 + c % 2][:, 0:T], ACT.Sigmoid)
                nc.scalar.copy(tmpv[:, c % 2, :], bank[4 * (c // 2 % 2) + c % 2][:, 0:T]).then_inc(gate_sig, 1)
            for n in range(4 * KC):
                kind, c = divmod(n, KC)
                act.wait_ge(proj, n + 1)
                src = bank[n % 4][:, 0:T]
                if kind == 0:
                    if c < 2:
                        act.wait_ge(glu_ready, KC - 1 + c)
                    else:
                        act.wait_ge(v_transposed, c - 1)
                    nc.scalar.activation(tmpc[:, c % 2, :], src, ACT.Gelu).then_inc(act_evac, 1)
                    if c >= 1:
                        copy_v(act, c - 1)
                elif kind == 1:
                    if c == 0:
                        copy_v(act, KC - 1)
                    if c == 0:
                        act.wait_ge(evac_early, 5)
                    nc.scalar.activation(uT[:, c, :], src, ACT.Gelu).then_inc(act_evac, 1)
                    if c == 0:
                        for h in range(2):
                            act.wait_ge(st_transposed, 4 * (h + 1))
                            nc.scalar.copy(st_rows[0:HIST, 0, h * 512:(h + 1) * 512], bank[6][0:HIST, :]
                                           ).then_inc(st_ready, 1)
                        for h in range(2):
                            act.wait_ge(st_transposed, 8 + 4 * (h + 1))
                            nc.scalar.copy(st_rows[:, 1, h * 512:(h + 1) * 512], bank[7][0:NS, :]
                                           ).then_inc(st_ready, 1)
                        act.wait_ge(st_ready, 4)
                        act.dma_start(out["conv_state_prompt"][0, 0], st_rows[0:HIST, 0, :]).then_inc(st_stored, 16)
                        for b in range(DB):
                            act.dma_start(out["conv_state_sample"][0, b, HIST - DS:HIST, :],
                                          st_rows[b * DS:(b + 1) * DS, 1, :]).then_inc(st_stored, 16)
                elif kind == 2:
                    if c == 0:
                        act.wait_ge(st_stored, 16 * (1 + DB))
                    if c == 2:
                        act.wait_ge(v_stats, 1)
                        root(ss[:, 8:10], mv[:, 0:2, 1], 1.0)
                        root(ss[0:NS, 10:11], mv[0:NS, 2, 1:2], 1.0)
                        act.wait_ge(centered, 1)
                        nc.scalar.activation(sq, conv, ACT.Square).then_inc(sq_ready, 1)
                    nc.scalar.activation(gaT[:, c, :], src, ACT.Sigmoid, bias=col(GATE_A, c)).then_inc(act_evac, 1)
                else:
                    if c == 0:
                        act.wait_ge(var_ready, 1)
                        root(dev_inv, bank[5][:, 0:T], 1.0)
                        act.wait_ge(v_normed, NT)
                    nc.scalar.activation(gbT[:, c, :], src, ACT.Sigmoid, bias=col(GATE_B, c)).then_inc(act_evac, 1)
            act.wait_ge(v_normed, NT)
            act.dma_start(out["chunk_v_sample"].rearrange("l b t d -> (l b t) d"), stage[0:NS, 2, :]
                          ).then_inc(v_stored, 16)
            act.wait_ge(conv_normed, 1)
            for c in range(KC):
                nc.scalar.activation(conv[:, c, :], conv[:, c, :], ACT.Silu, bias=col(LNC_B, c),
                                     scale=col(LNC_G, c)).then_inc(silu_done, 1)
            for c in range(KC):
                act.wait_ge(mo_ready, c + 1)
                if c >= 2:
                    act.wait_ge(mo_transposed, c - 1)
                nc.scalar.copy(tmpc[:, c % 2, :], bank[c % 4][:, 0:T]).then_inc(mo_evac, 1)
                if c == 5:
                    act.wait_ge(v_stored, 16)
                    act.wait_ge(x2_ready, KC // 2)
                    for tt in range(NT):
                        nc.scalar.activation(stage[:, tt, 0:D // 2], xt[:, tt, 0:D // 2], ACT.Square,
                                             accum_out=ss[:, 8 + tt:9 + tt]).then_inc(squared2, 1)
            load_root_table()
            act.wait_ge(x2_ready, KC)
            for tt in range(NT):
                nc.scalar.activation(stage[:, tt, D // 2:D], xt[:, tt, D // 2:D], ACT.Square,
                                     accum_out=ss[:, tt:tt + 1]).then_inc(squared2, 1)
            act.dma_start(bdown, a["b_down"][0]).then_inc(bdown_in, 16)
            act.dma_start(fing, a["norm_final_g"].rearrange("(l d) -> l d", l=1).to_broadcast([P, D])
                          ).then_inc(fing_in, 16)
            act.wait_ge(sums_added, 1)
            root(ss[:, 4:4 + NT], ss[:, 0:NT], 1.0 / D)
            for c in range(KC):
                act.wait_ge(x2_transposed, c + 1)
                nc.scalar.mul(hT[:, c, :], bank[c][:, 0:T], col(NORM_FFN, c)).then_inc(h2T_ready, 1)
            act.wait_ge(shifted, 1)
            nc.scalar.activation(gates[:], gates[:], ACT.Exp).then_inc(exped, 1)
            act.wait_ge(gT_ready, 1)
            nc.scalar.copy(gateT, bank[5][0:NE, 0:T]).then_inc(gT_evac, 1)
            act.wait_ge(items_known, 1)
            count = act.value_load(n_items[0:1, 0:1], min_val=NE, max_val=MAX_ITEMS)
            with act.Fori(0, count) as i:
                used = i * SLOTS
                act.wait_ge(slots_used, used + UP_SLOTS)
                nc.scalar.copy(raw_g, U0[:, :]).then_inc(raw_g_ready, 1)
                act.wait_ge(g1_ready, i + 1)
                nc.scalar.activation(sg, g1, ACT.Sigmoid, scale=ALPHA).then_inc(sig_ready, 1)
                act.wait_ge(slots_used, used + SLOTS)
                act.wait_ge(combined, i * NT + NT)
                nc.scalar.copy(out_sb, DN[:, :]).then_inc(out_ready, 1)
                act.wait_ge(combT_turned, i + 1)
                nc.scalar.copy(combT, XB[:, 0:NT * P]).then_inc(combT_ready, 1)
            load_root_table()
            for tt in range(NT):
                act.wait_ge(y_added, count * NT + (NT + tt + 1))
                nc.scalar.activation(stage[:, tt, :], xt[:, tt, :], ACT.Square, accum_out=ss[:, tt:tt + 1]
                                     ).then_inc(squared3, 1)
            act.wait_ge(squared3, NT)
            root(ss[:, 4:4 + NT], ss[:, 0:NT], 1.0 / D)

        @block.vector
        def _(dve):
            link = make_link(dve, dve_step)
            V = nc.vector

            V.memset(xt[NS:64, 2, :], 0.0).then_inc(pads_zero, 1)
            V.memset(xt[64:P, 2, :], 0.0).then_inc(pads_zero, 1)
            dve.wait_ge(const_ready, 5)
            V.tensor_copy(rep4[:], ident[0:DS, 0:DS].unsqueeze(1).to_broadcast([DS, DB, DS])
                          ).then_inc(ws_raw, 1)
            dve.wait_ge(pe_early, 1)
            V.tensor_copy(cols[:].rearrange("p v c -> p (v c)"), bank[7][:, 0:8 * KC]).then_inc(evac_early, 1)
            dve.wait_ge(rooted, 1)
            link(V.reciprocal(ss[:, 4:4 + NT], ss[:, 4:4 + NT]))
            for tt in range(NT):
                V.tensor_scalar(stage[:, tt, :], xt[:, tt, :], ss[:, 4 + tt:5 + tt], None, ALU.mult
                                ).then_inc(xs_ready, 1)
            dve.wait_ge(pe_early, 2)
            for c in range(KC):
                ins = V.tensor_copy(csample[:, c, :, 0:HIST],
                                    bank[4 + c // 2][:, (c % 2) * DB * HIST:(c % 2 + 1) * DB * HIST]
                                    .rearrange("p (b h) -> p b h", b=DB))
            ins.then_inc(evac_early, 1)
            dve.wait_ge(pe_early, 3)
            V.tensor_copy(convw[:], bank[4][:, 0:KC * W].rearrange("p (c k) -> p c k", c=KC)
                          ).then_inc(evac_early, 1)
            dve.wait_ge(pe_early, 4)
            V.tensor_copy(bupT[:].rearrange("p e f -> p f e"), bank[5][:, :].rearrange("p (f e) -> p f e", e=NE)
                          ).then_inc(evac_early, 1)
            dve.wait_ge(pe_early, 5)
            for h in range(2):
                ins = V.tensor_copy(WT[:, 4 * h:4 * h + 4, :],
                                    bank[6 + h][:, :].rearrange("p (g i) -> p g i", g=4))
            ins.then_inc(evac_early, 1)

            def select(column):
                for tt in range(NT):
                    ins = V.tensor_scalar(sel[:, tt, :], slot_ids[:, 0, :], tbl_rank[:, tt, bass.ds(column, 1)],
                                          None, ALU.is_equal)
                ins.then_inc(sel_ready, 1)

            def select_weighted(column):
                for tt in range(NT):
                    ins = V.tensor_scalar(comb[:, tt], slot_ids[:], tbl_rank[:, tt, bass.ds(column, 1)],
                                          tbl_gate[:, tt, bass.ds(column, 1)], ALU.is_equal, ALU.mult)
                ins.then_inc(comb_ready, 1)

            def take_x():
                V.tensor_tensor(xT, XB[:, :].rearrange("p (k t) -> p k t", k=KC),
                                cols[:, NORM_FFN, :].unsqueeze(2).to_broadcast([P, KC, BLK]), ALU.mult
                                ).then_inc(xT_ready, 1)

            def convolve(pair):
                for k in range(W):
                    for c in pair:
                        acc = conv[:, c, 0:SEQ]
                        if k == 0:
                            ins = V.tensor_scalar(acc, cprompt[:, c, 0:SEQ], convw[:, c, 0:1], col(CONV_B, c),
                                                  ALU.mult, ALU.add)
                        else:
                            dve.wait_ge(dve_step, link.count[0] - 1)
                            ins = V.scalar_tensor_tensor(acc, cprompt[:, c, k:k + SEQ], convw[:, c, k:k + 1], acc,
                                                         ALU.mult, ALU.add)
                        ins.then_inc(dve_step, 1)
                        link.count[0] += 1
            def convolve_sample(tiles):
                for c in tiles:
                    dve.wait_ge(prod_ready, DS * (c + 1))
                    tail = conv[:, c, SEQ:T]
                    V.tensor_reduce(tail, prod[:].rearrange("p b t k -> p (b t) k"), AX.X, ALU.add
                                    ).then_inc(prod_used, 1)
                    dve.wait_ge(prod_used, c + 1)
                    V.tensor_scalar(tail, tail, col(CONV_B, c), None, ALU.add).then_inc(conv_done, 1)

            dve.wait_ge(history_zero, 1)
            for pair in range(KC // 2):
                dve.wait_ge(glu_ready, 2 * pair + 2)
                convolve((2 * pair, 2 * pair + 1))
                if pair == 2:
                    convolve_sample(range(0, 3))
            convolve_sample(range(3, KC))
            dve.wait_ge(v_rows, 2 * KC)
            for tt in range(NT):
                r = ROWS[tt]
                for h in range(2):
                    link(V.bn_stats(bnst[0:r, tt, h, :], stage[0:r, tt, h * 512:(h + 1) * 512]))
                ins = V.bn_aggr(mv[0:r, tt, :], bnst[0:r, tt, :, :])
                if tt < NT - 1:
                    link(ins)
            ins.then_inc(v_stats, 1)
            dve.wait_ge(mean_ready, 1)
            ins = V.tensor_tensor(conv, conv, bank[4][:, 0:T].unsqueeze(1).to_broadcast([P, KC, T]), ALU.subtract)
            ins.then_inc(centered, 1)
            dve.wait_ge(rooted, 3)
            link(V.reciprocal(ss[:, 8:10], ss[:, 8:10]))
            link(V.reciprocal(ss[0:NS, 10:11], ss[0:NS, 10:11]))
            dve.wait_ge(lnv_in, 48)
            for tt in range(NT):
                r = ROWS[tt]
                row = stage[0:r, tt, :]
                link(V.tensor_scalar(row, row, mv[0:r, tt, 0:1], ss[0:r, 8 + tt:9 + tt], ALU.subtract, ALU.mult))
                link(V.tensor_tensor(row, row, lnv_g[0:r], ALU.mult))
                V.tensor_tensor(row, row, lnv_b[0:r], ALU.add).then_inc(v_normed, 1)
            dve.wait_ge(ws_ready, 1)
            ps = bank[6][0:NS, 0:G * DS].rearrange("p (g i) -> p g i", g=G)
            for b in range(DB):
                ins = V.tensor_scalar(WS[:, :, b * DS:(b + 1) * DS], ps, bmask[:, b:b + 1], None, ALU.mult)
            ins.then_inc(ws_raw, 1)
            dve.wait_ge(rooted, 4)
            link(V.reciprocal(dev_inv, dev_inv))
            V.tensor_tensor(conv, conv, dev_inv.unsqueeze(1).to_broadcast([P, KC, T]), ALU.mult).then_inc(conv_normed, 1)
            for g in range(G):
                dve.wait_ge(sp_ready, g + 1)
                b = bank[4 + g % 4]
                sp = sq[:, g, :]
                V.tensor_tensor(sp[:, 0:SEQ].rearrange("p (c i) -> p c i", c=2),
                                b[:, 0:SEQ].rearrange("p (c i) -> p c i", c=2),
                                spb[:, g:g + 1, :].to_broadcast([P, 2, P]), ALU.add)
                V.tensor_tensor(sp[:, SEQ:T].rearrange("p (b i) -> p b i", b=DB),
                                b[:, SEQ:T].rearrange("p (b i) -> p b i", b=DB),
                                spb[:, g:g + 1, 0:DS].to_broadcast([P, DB, DS]), ALU.add).then_inc(sp_evac, 1)
                dve.wait_ge(sp_evac, 2 * g + 1)
                V.tensor_tensor(uT[:, g, :], uT[:, g, :], sp, ALU.mult).then_inc(sp_evac, 1)
            for c in range(KC):
                dve.wait_ge(yb_ready, c + 1)
                V.scalar_tensor_tensor(gbT[:, c, :], bank[c % 4][:, 0:T], col(B_B, c), gbT[:, c, :],
                                       ALU.add, ALU.mult).then_inc(yb_evac, 1)
            for c in range(KC):
                dve.wait_ge(ya_ready, c + 1)
                V.tensor_tensor(gaT[:, c, :], bank[c % 4][:, 0:T], gaT[:, c, :], ALU.mult).then_inc(ya_evac, 1)
                dve.wait_ge(ya_evac, 2 * c + 1)
                V.tensor_tensor(gaT[:, c, :], gaT[:, c, :], gbT[:, c, :], ALU.add).then_inc(ya_evac, 1)
            for c in range(KC):
                dve.wait_ge(mo_transposed, c + 1)
                b = bank[4 + c % 4]
                x01 = xt[:, 0:2, c * P:(c + 1) * P]
                V.tensor_tensor(x01, x01, b[:, 0:2 * P].rearrange("p (t d) -> p t d", t=2), ALU.add)
                x2 = xt[0:NS, 2, c * P:(c + 1) * P]
                V.tensor_tensor(x2, x2, b[0:NS, 2 * P:3 * P], ALU.add).then_inc(x2_ready, 1)
            dve.wait_ge(squared2, 2 * NT)
            V.tensor_tensor(ss[:, 0:NT], ss[:, 0:NT], ss[:, 8:8 + NT], ALU.add).then_inc(sums_added, 1)
            dve.wait_ge(rooted, 5)
            link(V.reciprocal(ss[:, 4:4 + NT], ss[:, 4:4 + NT]))
            for tt in range(NT):
                V.tensor_scalar(stage[:, tt, :], xt[:, tt, :], ss[:, 4 + tt:5 + tt], None, ALU.mult
                                ).then_inc(xs2_ready, 1)
            link(V.memset(lx[:, :, NE:NE + 8], SENTINEL))
            link(V.memset(want8[:, :, TOPK:8], SENTINEL))
            link(V.memset(lx[:, 2, 0:NE], 0.0))
            dve.wait_ge(wr_in, 32)
            dve.wait_ge(logits_ready, 1)
            lps = bank[0][:, 0:NT * NE].rearrange("p (t e) -> p t e", t=NT)
            V.tensor_tensor(lx[:, 0:2, 0:NE], lps[:, 0:2], br[:].unsqueeze(1).to_broadcast([P, 2, NE]), ALU.add)
            link(V.tensor_tensor(lx[0:NS, 2, 0:NE], lps[0:NS, 2], br[0:NS, :], ALU.add))
            for tt in range(NT):
                link(V.max(top8[:, tt, :], lx[:, tt, 0:NE]))
            link(V.tensor_copy(want8[:, :, 0:TOPK], top8[:, :, 0:TOPK]))
            V.tensor_tensor(gates[:], lx[:, :, 0:NE], top8[:, :, 0:1].to_broadcast([P, NT, NE]), ALU.subtract
                            ).then_inc(shifted, 1)
            for tt in range(NT):
                link(V.match_replace(lr[:, tt, :], want8[:, tt, :], lx[:, tt, :], -SENTINEL))
            link(V.tensor_tensor(mask[:], lr[:, :, 0:NE], lx[:, :, 0:NE], ALU.not_equal))
            dve.wait_ge(exped, 1)
            link(V.tensor_tensor(gates[:], gates[:], mask[:], ALU.mult))
            link(V.tensor_reduce(ss[:, 12:12 + NT], gates[:], AX.X, ALU.add))
            link(V.reciprocal(ss[:, 12:12 + NT], ss[:, 12:12 + NT]))
            link(V.tensor_tensor(gates[:], gates[:], ss[:, 12:12 + NT].unsqueeze(2).to_broadcast([P, NT, NE]), ALU.mult))
            for lo, hi in ((NS, 64), (64, P)):
                V.memset(gates[lo:hi, 2, :], 0.0)
                link(V.memset(mask[lo:hi, 2, :], 0.0))
            V.memset(out_sb, 0.0).then_inc(out_ready, 1)
            V.memset(combT, 0.0).then_inc(combT_ready, 1)
            V.tensor_scalar(rankm[:], mask[:], ABSENT, -ABSENT, ALU.mult, ALU.add).then_inc(routed, 1)
            dve.wait_ge(rank_ready, 1)
            rps = bank[1][:, 0:NT * NE].rearrange("p (t e) -> p t e", t=NT)
            link(V.tensor_tensor(rankm[:], rankm[:], rps, ALU.add))
            for r in range(MAX_ROUNDS):
                V.tensor_scalar(tbl_rank[:, :, r * NE:(r + 1) * NE], rankm[:], -float(BLK * r), None, ALU.add)
                ins = V.tensor_copy(tbl_gate[:, :, r * NE:(r + 1) * NE], gates[:])
            link(ins)
            select(0)
            dve.wait_ge(col_ids_ready, 1)
            for r in range(1, MAX_ROUNDS):
                ins = V.tensor_scalar(need[:, r - 1, :], bank[2][:, 0:NE], float(BLK * r), None, ALU.is_gt)
            link(ins)
            src, dst, step_by = need, pos_a, 1
            while step_by < NE:
                V.tensor_copy(dst[:, :, 0:step_by], src[:, :, 0:step_by])
                link(V.tensor_tensor(dst[:, :, step_by:NE], src[:, :, step_by:NE], src[:, :, 0:NE - step_by], ALU.add))
                src, dst, step_by = dst, (pos_b if dst is pos_a else pos_a), 2 * step_by
            link(V.tensor_scalar(src[:, 0, :], src[:, 0, :], float(NE), None, ALU.add))
            for r in range(1, MAX_ROUNDS - 1):
                link(V.tensor_scalar(src[:, r, :], src[:, r, :], src[:, r - 1, NE - 1:NE], None, ALU.add))
            V.tensor_copy(n_items[:], src[:, MAX_ROUNDS - 2, NE - 1:NE])
            link(V.tensor_scalar(dst, src, item_ids[:, 0:1], 1.0, ALU.subtract, ALU.is_equal))
            link(V.tensor_tensor(dst, dst, need, ALU.mult))
            link(V.tensor_tensor(dst, dst, col_ids, ALU.mult))
            link(V.tensor_reduce(item_row, dst, AX.XY, ALU.add))
            V.tensor_tensor(item_row, item_row, item_ids[:, 1:2], ALU.add).then_inc(listed, 1)
            add_bias_rows(dve, 0)
            add_bias_rows(dve, 1)
            dve.wait_ge(gathered, 1)
            take_x()
            dve.wait_ge(list_turned, 1)
            V.tensor_copy(items[:], bank[3][0:1, 0:P]).then_inc(items_known, 1)
            add_bias_rows(dve, 2)
            dve.wait_ge(items_known, 1)
            count = dve.value_load(n_items[0:1, 0:1], min_val=NE, max_val=MAX_ITEMS)
            base0 = link.count[0]
            with dve.Fori(0, count) as i:
                n_links = [0]

                def step(ins):
                    n_links[0] += 1
                    ins.then_inc(dve_step, 1)
                    dve.wait_ge(dve_step, i * LINKS + (base0 + n_links[0]))

                column = dve.value_load(items[0:1, bass.ds(i, 1)], min_val=0, max_val=TBL - 1)
                column_next = dve.value_load(items[0:1, bass.ds(i + 1, 1)], min_val=0, max_val=TBL - 1)
                dve.wait_ge(gathered, i + 1)
                select(column_next)
                dve.wait_ge(combT_ready, i + 1)
                select_weighted(column)
                dve.wait_ge(slots_used, i * SLOTS + UP_SLOTS)
                V.tensor_copy(raw_u, U1[:, :]).then_inc(raw_u_ready, 1)

                def bias(z, q):
                    f = (2 * z + q) * 4
                    return bupT[:, bass.ds(column & (NE - 1), 1), f:f + 4].rearrange("p e c -> p (e c)") \
                        .unsqueeze(2).to_broadcast([P, 4, BLK])

                def shaped(t):
                    return t.rearrange("p (c q t) -> p c q t", c=4, q=2)

                for z, (src, dst) in enumerate(((T0, g1), (T1, u1))):
                    dve.wait_ge(turned, i * 2 + (z + 1))
                    for q in range(2):
                        ins = V.tensor_tensor(shaped(dst)[:, :, q, :], shaped(src[:, :])[:, :, q, :],
                                              bias(z, q), ALU.add)
                    if z == 0:
                        step(ins)
                        V.tensor_scalar(g1, g1, LIMIT, None, ALU.min).then_inc(g1_ready, 1)
                    else:
                        ins.then_inc(turned_read, 1)
                        dve.wait_ge(turned_read, i + 1)
                        step(V.tensor_scalar(u1, u1, LIMIT, -LIMIT, ALU.min, ALU.max))
                dve.wait_ge(sig_ready, i + 1)
                step(V.tensor_tensor(gs, g1, sg, ALU.mult))
                V.scalar_tensor_tensor(actT, u1, 1.0, gs, ALU.add, ALU.mult).then_inc(act_ready, 1)
                dve.wait_ge(gathered, i + 2)
                take_x()
                add_outputs(dve, i * NT)
                assert n_links[0] == LINKS
            add_outputs(dve, count * NT)
            dve.wait_ge(fing_in, 16)
            base1 = count * LINKS + base0
            dve.wait_ge(rooted, 6)
            V.reciprocal(ss[:, 4:4 + NT], ss[:, 4:4 + NT]).then_inc(dve_step, 1)
            dve.wait_ge(dve_step, base1 + 1)
            for tt in range(NT):
                r = ss[:, 4 + tt:5 + tt]
                V.scalar_tensor_tensor(xt[:, tt, :], xt[:, tt, :], r, fing, ALU.mult, ALU.mult).then_inc(y_ready, 1)

        @block.tensor
        def _(pe):
            mm = nc.tensor.matmul

            def tr(dst, src):
                n = src.shape[0]
                return nc.tensor.transpose(dst, src, ident[0:n, 0:n])

            pe.wait_ge(const_ready, 5)
            pe.wait_ge(vec_in, 16 * 8)
            tr(bank[7][:, 0:8 * KC], vecrows[:]).then_inc(pe_early, 1)
            pe.wait_ge(evac_early, 1)
            pe.wait_ge(xs_ready, NT)
            for c in range(KC):
                for tt in range(NT):
                    r = ROWS[tt]
                    ins = tr(bank[c][:, tt * P:tt * P + r], stage[0:r, tt, c * P:(c + 1) * P])
                ins.then_inc(x_transposed, 1)

            def gather(tiles):
                for k in tiles:
                    for tt in range(NT):
                        ins = mm(XB[:, k * BLK:(k + 1) * BLK], stage[:, tt, k * P:(k + 1) * P], sel[:, tt, :],
                                 start=tt == 0, stop=tt == NT - 1)
                return ins

            def combine(tt):
                for q in range(2):
                    ins = mm(row_banks[tt][q][:, :], combT[q * BLK:(q + 1) * BLK, tt * P:(tt + 1) * P],
                             out_sb[q * BLK:(q + 1) * BLK, :], start=True, stop=True)
                ins.then_inc(combined, 1)

            def project(n, h, dst, src):
                w = ring[:, n % SLOTS, :].rearrange("p (k n) -> p k n", k=KC)
                if h == 0:
                    pe.wait_ge(slot_full[n % SLOTS], 16 * (n // SLOTS + 1))
                for k in range(KC):
                    ins = mm(dst[:, 0:T], w[:, k, h * P:(h + 1) * P], src[:, k, :], start=k == 0, stop=k == KC - 1)
                return ins

            pe.wait_ge(hT_ready, KC)
            for j in range(KC // 2):
                if j >= 2:
                    pe.wait_ge(gate_sig, 2 * (j - 1))
                for part in range(2):
                    n = 2 * j + part
                    for h in range(2):
                        project(n, h, bank[4 * (j % 2) + 2 * part + h], hT[:]).then_inc(c_proj, 1)
                if j == 0:
                    pe.wait_ge(cache_in, 32)
                    for c in range(KC):
                        for h in range(2):
                            lo = ((c % 2) * 2 + h) * 4 * HIST
                            ins = tr(bank[4 + c // 2][:, lo:lo + 4 * HIST], cache_rows[:, h, c * P:(c + 1) * P])
                    ins.then_inc(pe_early, 1)
                    pe.wait_ge(evac_early, 2)
                    pe.wait_ge(cw_in, 16)
                    for c in range(KC):
                        ins = tr(bank[4][:, c * W:(c + 1) * W], cw_rows[:, c * P:(c + 1) * P])
                    ins.then_inc(pe_early, 1)
                    pe.wait_ge(bup_in, 16)
                    for f in range(2 * KC):
                        ins = tr(bank[5][:, f * NE:(f + 1) * NE], bup_rows[:, f * P:(f + 1) * P])
                    ins.then_inc(pe_early, 1)
                    pe.wait_ge(wsp_in, 16)
                    for g in range(G):
                        ins = tr(bank[6 + g // 4][:, (g % 4) * P:(g % 4 + 1) * P], wsp[:, g, :])
                    ins.then_inc(pe_early, 1)
                    pe.wait_ge(evac_early, 5)
            pe.wait_ge(gate_sig, KC)
            for n in range(4 * KC):
                kind, c = divmod(n, KC)
                if n >= 4:
                    pe.wait_ge(act_evac, n - 3)
                project(8 + n // 2, n % 2, bank[n % 4], hT[:]).then_inc(proj, 1)
                if 1 <= n <= KC:
                    turn_v(pe, tr, n - 1)
                if n == KC:
                    pe.wait_ge(tail_packed, 1)
                    for q in range(2):
                        for c2 in range(KC):
                            if c2 == 4:
                                pe.wait_ge(st_ready, 1) if q == 0 else pe.wait_ge(st_ready, 3)
                            dst = bank[6 + q][0:(HIST, NS)[q], (c2 % 4) * P:(c2 % 4 + 1) * P]
                            src = cprompt[:, c2, SEQ:SEQ + HIST] if q == 0 else glu_tail[:, c2, :]
                            nc.tensor.transpose(dst, src, ident[:]).then_inc(st_transposed, 1)
                if n == 2 * KC + 1:
                    pe.wait_ge(conv_done, KC)
                    pe.wait_ge(v_rows, 2 * KC)
                    for c2 in range(KC):
                        ins = mm(bank[4][:, 0:T], mean_w[:], conv[:, c2, :], start=c2 == 0, stop=c2 == KC - 1)
                    ins.then_inc(mean_ready, 1)
                    pe.wait_ge(wt_masked, 1)
                    pe.wait_ge(ws_raw, 1)
                    pe.wait_ge(st_ready, 4)
                    mm(bank[6][0:NS, 0:G * DS].rearrange("p (g i) -> p g i", g=G), rep4[:].rearrange("p b j -> p (b j)"),
                       WT[0:DS, :, 0:DS], start=True, stop=True).then_inc(ws_ready, 1)
                if n == 3 * KC - 1:
                    pe.wait_ge(sq_ready, 1)
                    for c2 in range(KC):
                        ins = mm(bank[5][:, 0:T], mean_w[:], sq[:, c2, :], start=c2 == 0, stop=c2 == KC - 1)
                    ins.then_inc(var_ready, 1)
            pe.wait_ge(v_normed, NT)
            pe.wait_ge(ws_raw, 2)
            pe.wait_ge(conv_normed, 1)
            for g in range(G):
                if g >= 4:
                    pe.wait_ge(sp_evac, 2 * (g - 4) + 1)
                b = bank[4 + g % 4]
                for c in range(2):
                    mm(b[:, c * P:(c + 1) * P], stage[:, c, g * P:(g + 1) * P], WT[:, g, :], start=True, stop=True)
                mm(b[:, SEQ:T], stage[0:NS, 2, g * P:(g + 1) * P], WS[:, g, :], start=True, stop=True
                   ).then_inc(sp_ready, 1)
            for m in range(KC):
                if m == 0:
                    pe.wait_ge(silu_done, KC)
                if m < 4:
                    pe.wait_ge(act_evac, 4 * KC - 3 + m)
                else:
                    pe.wait_ge(yb_evac, m - 3)
                project(24 + m // 2, m % 2, bank[m % 4], conv).then_inc(yb_ready, 1)
            for m in range(KC):
                if m == 0:
                    pe.wait_ge(sp_evac, 2 * G)
                if m < 4:
                    pe.wait_ge(yb_evac, KC - 3 + m)
                else:
                    pe.wait_ge(ya_evac, 2 * (m - 4) + 1)
                project(28 + m // 2, m % 2, bank[m % 4], uT).then_inc(ya_ready, 1)
            for m in range(KC):
                if m == 0:
                    pe.wait_ge(ya_evac, 2 * KC)
                if m >= 4:
                    pe.wait_ge(mo_evac, m - 3)
                project(32 + m // 2, m % 2, bank[m % 4], gaT).then_inc(mo_ready, 1)
                if m >= 1:
                    turn_mixed(pe, tr, m - 1)
            turn_mixed(pe, tr, KC - 1)
            pe.wait_ge(xs2_ready, NT)
            pe.wait_ge(mo_evac, KC)
            for c in range(KC):
                for tt in range(NT):
                    r = ROWS[tt]
                    ins = tr(bank[c][:, tt * P:tt * P + r], stage[0:r, tt, c * P:(c + 1) * P])
                ins.then_inc(x2_transposed, 1)
            pe.wait_ge(h2T_ready, KC)
            pe.wait_ge(wr_in, 32)
            for tt in range(NT):
                for k in range(KC):
                    ins = mm(bank[0][0:ROWS[tt], tt * NE:(tt + 1) * NE], hT[:, k, token_slices(tt)], wr[:, k, :],
                             start=k == 0, stop=k == KC - 1)
            ins.then_inc(logits_ready, 1)
            pe.wait_ge(routed, 1)
            for tt in range(NT):
                for t2 in range(tt + 1):
                    ins = mm(bank[1][:, tt * NE:(tt + 1) * NE], (below if t2 == tt else ones)[:], mask[:, t2, :],
                             start=t2 == 0, stop=t2 == tt)
            for t2 in range(NT):
                ins = mm(bank[2][:, 0:NE], ones[:], mask[:, t2, :], start=t2 == 0, stop=t2 == NT - 1)
            ins.then_inc(rank_ready, 1)
            for tt in range(NT):
                r = ROWS[tt]
                ins = tr(bank[5][0:NE, tt * P:tt * P + r], gates[0:r, tt, :])
            ins.then_inc(gT_ready, 1)
            pe.wait_ge(gT_evac, 1)
            pe.wait_ge(bdown_in, 16)
            for tt in range(NT):
                if tt == 2:
                    pe.wait_ge(sel_ready, 1)
                    gather(range(KC)).then_inc(gathered, 1)
                    pe.wait_ge(listed, 1)
                    tr(bank[3][0:1, 0:P], item_row).then_inc(list_turned, 1)
                    pe.wait_ge(y_added, 1)
                for h in range(2):
                    ins = mm(bias_banks[tt][h][0:ROWS[tt], :], gateT[:, token_slices(tt)],
                             bdown[:, h * 512:(h + 1) * 512], start=True, stop=True)
                ins.then_inc(bd_ready, 1)
            pe.wait_ge(items_known, 1)
            count = pe.value_load(n_items[0:1, 0:1], min_val=NE, max_val=MAX_ITEMS)
            with pe.Fori(0, count) as i:
                fills = i * 16 + 16 * (FILLS + 1)
                pe.wait_ge(xT_ready, i + 1)
                pe.wait_ge(y_added, i * NT + 2)
                for k in range(UP_SLOTS):
                    pe.wait_ge(slot_full[k], fills)
                    for z, dst in enumerate((U0, U1)):
                        for q in range(2):
                            lo = z * D + q * 512
                            ins = mm(dst[q * BLK:(q + 1) * BLK, :], xT[:, k, :], ring[:, k, lo:lo + 512],
                                     start=k == 0, stop=k == UP_SLOTS - 1)
                    ins.then_inc(slots_used, 1)
                pe.wait_ge(sel_ready, i + 2)
                pe.wait_ge(combT_ready, i + 1)
                gather(range(KC // 2))
                pe.wait_ge(y_added, i * NT + NT)
                for src, dst, ready in ((raw_g, T0, raw_g_ready), (raw_u, T1, raw_u_ready)):
                    pe.wait_ge(ready, i + 1)
                    for c in range(4):
                        ins = tr(dst[:, c * P:(c + 1) * P], src[:, c * P:(c + 1) * P])
                    ins.then_inc(turned, 1)
                gather(range(KC // 2, KC)).then_inc(gathered, 1)
                pe.wait_ge(out_ready, i + 1)
                combine(0)
                combine(1)
                pe.wait_ge(turned_read, i + 1)
                combine(2)
                pe.wait_ge(act_ready, i + 1)
                for j in range(SLOTS - UP_SLOTS):
                    k = UP_SLOTS + j
                    pe.wait_ge(slot_full[k], fills)
                    for h in range(2):
                        f = 2 * j + h
                        lhsT = actT.rearrange("p (c q t) -> p c q t", c=4, q=2)[:, f % 4, f // 4, :]
                        for q in range(2):
                            lo = h * D + q * 512
                            ins = mm(DN[q * BLK:(q + 1) * BLK, :], lhsT, ring[:, k, lo:lo + 512],
                                     start=f == 0, stop=f == KC - 1)
                    ins.then_inc(slots_used, 1)
                pe.wait_ge(xT_ready, i + 2)
                pe.wait_ge(comb_ready, i + 1)
                for tt in range(NT):
                    ins = tr(XB[:, tt * P:(tt + 1) * P], comb[:, tt].rearrange("p q j -> p (q j)"))
                ins.then_inc(combT_turned, 1)
            pe.wait_ge(out_ready, count + 1)
            pe.wait_ge(combT_ready, count + 1)
            pe.wait_ge(y_added, count * NT + NT)
            for tt in range(NT):
                combine(tt)


INPUTS = ["x_prompt", "x_sample", "cache_conv", "norm_mix_g", "w_in", "ln_v_g", "ln_v_b", "w_spatial", "b_spatial",
          "w_branch_a", "conv_w", "conv_b", "ln_conv_g", "ln_conv_b", "w_branch_b", "b_branch_b", "b_gate_a",
          "b_gate_b", "w_out", "norm_ffn_g", "w_router", "b_router", "w_up", "b_up", "w_down", "b_down",
          "norm_final_g"]
OUTPUTS = {"y_prompt": (1, SEQ, D), "y_sample": (DB, DS, D), "conv_state_prompt": (1, 1, HIST, D),
           "conv_state_sample": (1, DB, HIST, D), "chunk_v_sample": (1, DB, DS, D)}


def kernel(**inputs):
    import numpy as np
    import concourse.bacc as bacc
    from concourse.bass_utils import run_bass_kernel_spmd

    nc = bacc.Bacc("TRN2", target_bir_lowering=False, num_devices=1)
    arrays, a, out = {}, {}, {}
    for name in INPUTS:
        x = np.ascontiguousarray(inputs[name])
        arrays[f"in_{name}"] = x
        a[name] = nc.dram_tensor(f"in_{name}", x.shape, F32, kind="ExternalInput").ap()
    for name, shape in OUTPUTS.items():
        out[name] = nc.dram_tensor(f"out_{name}", shape, F32, kind="ExternalOutput").ap()
    hybrid_layer(nc, a, out)
    result = run_bass_kernel_spmd(nc, [arrays], core_ids=[0]).results[0]
    return tuple(result[f"out_{name}"] for name in OUTPUTS)
```
